# Optimizing a Trainium2 kernel written in Bass

```python
import math
import jax, jax.numpy as jnp
from jax import lax
import numpy as np

D_MODEL = 1024
BATCH = 1
SEQ = 512
DEPTH = 1
DEC_BATCH = 1
DEC_SEQ = 256
PAST_LEN = 128

HEAD_DIM = 64
N_HEADS_A = 8
N_HEADS_B = 8
N_KV_B = 2
WIDTH_A = N_HEADS_A * HEAD_DIM
WIDTH_B = N_HEADS_B * HEAD_DIM
KV_WIDTH_B = N_KV_B * HEAD_DIM
MIX_WIDTH = WIDTH_A + WIDTH_B
DILATED_PATTERNS = ((128, 1), (512, 4), (2048, 16))
GRID_W = 64
ROPE_THETA = 10000.0
Q_BLOCK = 128
LN_EPS = 1e-5
RMS_EPS = 1e-6
NEG_BIG = -1e30
DEEPNORM_ALPHA = (2.0 * DEPTH) ** 0.25
DEEPNORM_BETA = (8.0 * DEPTH) ** -0.25
IN_SIZES = (WIDTH_A, WIDTH_A, WIDTH_A, WIDTH_A, WIDTH_B, KV_WIDTH_B, KV_WIDTH_B, WIDTH_B)
IN_WIDTH = 4 * WIDTH_A + 2 * WIDTH_B + 2 * KV_WIDTH_B
IN_SPLITS = tuple(int(v) for v in np.cumsum(IN_SIZES)[:-1])

kernel_name = "hymba_dilated_gqa_axial_encoder"

def _rope_cos_sin(pos, dim):
    inv_freq = 1.0 / (ROPE_THETA ** (jnp.arange(0, dim, 2, dtype=jnp.float32) / dim))
    ang = pos.astype(jnp.float32)[:, None] * inv_freq[None, :]
    ang = jnp.concatenate([ang, ang], axis=-1)
    return jnp.cos(ang), jnp.sin(ang)

def _rope(x, cos, sin):
    xf = x.astype(jnp.float32)
    x1, x2 = jnp.split(xf, 2, axis=-1)
    rot = jnp.concatenate([-x2, x1], axis=-1)
    return (xf * cos[None, :, None, :] + rot * sin[None, :, None, :]).astype(x.dtype)

def _axial_rope(x, row, col):
    half = x.shape[-1] // 2
    cr, sr = _rope_cos_sin(row, half)
    cc, sc = _rope_cos_sin(col, half)
    return jnp.concatenate([_rope(x[..., :half], cr, sr), _rope(x[..., half:], cc, sc)], axis=-1)

def _rms_norm_heads(x, g):
    xf = x.astype(jnp.float32)
    xf = xf * lax.rsqrt(jnp.mean(xf * xf, axis=-1, keepdims=True) + RMS_EPS)
    return (xf * g.astype(jnp.float32)).astype(x.dtype)

def _dilated_attention(q, k, v):
    b, n, h, dh = q.shape
    scale = dh ** -0.5
    nb = n // Q_BLOCK
    qb = q.reshape(b, nb, Q_BLOCK, h, dh).transpose(1, 0, 2, 3, 4)
    starts = jnp.arange(nb, dtype=jnp.int32) * Q_BLOCK

    def block(args):
        q_blk, start = args
        qpos = start + jnp.arange(Q_BLOCK, dtype=jnp.int32)
        lses, outs = [], []
        for window, dil in DILATED_PATTERNS:
            half = window // (2 * dil)
            offs = dil * jnp.arange(-half, half + 1, dtype=jnp.int32)
            kpos = qpos[:, None] + offs[None, :]
            valid = (kpos >= 0) & (kpos < n)
            kidx = jnp.clip(kpos, 0, n - 1)
            kg = k[:, kidx]
            vg = v[:, kidx]
            s = jnp.einsum('bqhd,bqlhd->bhql', q_blk, kg,
                           preferred_element_type=jnp.float32) * scale
            s = jnp.where(valid[None, None], s, NEG_BIG)
            m = jnp.max(s, axis=-1, keepdims=True)
            p = jnp.exp(s - m)
            den = jnp.sum(p, axis=-1, keepdims=True)
            o = jnp.einsum('bhql,bqlhd->bqhd', p, vg.astype(jnp.float32))
            o = o / jnp.transpose(den, (0, 2, 1, 3))
            lse = jnp.transpose((m + jnp.log(den))[..., 0], (0, 2, 1))
            lses.append(lse)
            outs.append(o)
        w = jax.nn.softmax(jnp.stack(lses, axis=0), axis=0)
        out = jnp.sum(w[..., None] * jnp.stack(outs, axis=0), axis=0)
        return out.astype(q.dtype)

    out = lax.map(block, (qb, starts))
    return out.transpose(1, 0, 2, 3, 4).reshape(b, n, h, dh)

def _gqa_attention(q, k, v):
    b, n, hq, dh = q.shape
    hkv = k.shape[2]
    g = hq // hkv
    scale = dh ** -0.5
    nb = n // Q_BLOCK
    qb = q.reshape(b, nb, Q_BLOCK, hkv, g, dh).transpose(1, 0, 2, 3, 4, 5)

    def block(q_blk):
        s = jnp.einsum('bqkgd,bskd->bkgqs', q_blk, k,
                       preferred_element_type=jnp.float32) * scale
        p = jax.nn.softmax(s, axis=-1)
        o = jnp.einsum('bkgqs,bskd->bqkgd', p, v.astype(jnp.float32))
        return o.astype(q.dtype)

    out = lax.map(block, qb)
    return out.transpose(1, 0, 2, 3, 4, 5).reshape(b, n, hq, dh)

def _layer_norm(x, g, b):
    xf = x.astype(jnp.float32)
    mu = jnp.mean(xf, axis=-1, keepdims=True)
    var = jnp.mean(jnp.square(xf - mu), axis=-1, keepdims=True)
    y = (xf - mu) * lax.rsqrt(var + LN_EPS) * g.astype(jnp.float32) + b.astype(jnp.float32)
    return y.astype(x.dtype)

def _layer(x, w_in, w_out, q_norm, k_norm, ln_g, ln_b):
    b, n, _ = x.shape
    rows = n // GRID_W
    pos = jnp.arange(n, dtype=jnp.int32)
    row = jnp.repeat(jnp.arange(rows, dtype=jnp.int32), GRID_W)
    col = jnp.tile(jnp.arange(GRID_W, dtype=jnp.int32), rows)

    h = jnp.einsum('bnd,de->bne', x, w_in)
    qa, ka, va, ga, qb, kb, vb, gb = jnp.split(h, IN_SPLITS, axis=-1)

    cos, sin = _rope_cos_sin(pos, HEAD_DIM)
    qa = _rope(qa.reshape(b, n, N_HEADS_A, HEAD_DIM), cos, sin)
    ka = _rope(ka.reshape(b, n, N_HEADS_A, HEAD_DIM), cos, sin)
    va = va.reshape(b, n, N_HEADS_A, HEAD_DIM)
    out_a = _dilated_attention(qa, ka, va).reshape(b, n, WIDTH_A) * jax.nn.silu(ga)

    qb = _axial_rope(_rms_norm_heads(qb.reshape(b, n, N_HEADS_B, HEAD_DIM), q_norm), row, col)
    kb = _axial_rope(_rms_norm_heads(kb.reshape(b, n, N_KV_B, HEAD_DIM), k_norm), row, col)
    vb = vb.reshape(b, n, N_KV_B, HEAD_DIM)
    out_b = _gqa_attention(qb, kb, vb).reshape(b, n, WIDTH_B) * jax.nn.silu(gb)

    f = jnp.einsum('bne,ed->bnd', jnp.concatenate([out_a, out_b], axis=-1), w_out)
    return _layer_norm(DEEPNORM_ALPHA * x + f, ln_g, ln_b)

def setup_inputs(seed: int = 0) -> dict:
    key = jax.random.key(seed)
    ks = jax.random.split(key, 8)
    x_prompt = jax.random.normal(ks[0], (BATCH, SEQ, D_MODEL), jnp.float32)
    x_sample = jax.random.normal(ks[1], (DEC_BATCH, DEC_SEQ, D_MODEL), jnp.float32)
    col_scale = np.concatenate([
        np.ones(WIDTH_A), np.ones(WIDTH_A), np.full(WIDTH_A, DEEPNORM_BETA), np.ones(WIDTH_A),
        np.ones(WIDTH_B), np.ones(KV_WIDTH_B), np.full(KV_WIDTH_B, DEEPNORM_BETA), np.ones(WIDTH_B),
    ]).astype(np.float32)
    w_in = jax.random.normal(ks[2], (DEPTH, D_MODEL, IN_WIDTH), jnp.float32) * (D_MODEL ** -0.5)
    w_in = w_in * jnp.asarray(col_scale)[None, None, :]
    w_out = jax.random.normal(ks[3], (DEPTH, MIX_WIDTH, D_MODEL), jnp.float32) * (MIX_WIDTH ** -0.5) * DEEPNORM_BETA
    q_norm = 1.0 + 0.02 * jax.random.normal(ks[4], (DEPTH, HEAD_DIM), jnp.float32)
    k_norm = 1.0 + 0.02 * jax.random.normal(ks[5], (DEPTH, HEAD_DIM), jnp.float32)
    ln_g = 1.0 + 0.02 * jax.random.normal(ks[6], (DEPTH, D_MODEL), jnp.float32)
    ln_b = 0.02 * jax.random.normal(ks[7], (DEPTH, D_MODEL), jnp.float32)
    return {"x_prompt": x_prompt, "x_sample": x_sample, "w_in": w_in, "w_out": w_out,
            "q_norm": q_norm, "k_norm": k_norm, "ln_g": ln_g, "ln_b": ln_b}

def reference(x_prompt, x_sample, w_in, w_out, q_norm, k_norm, ln_g, ln_b):
    y_prompt = x_prompt
    y_sample = x_sample
    for i in range(DEPTH):
        y_prompt = _layer(y_prompt, w_in[i], w_out[i], q_norm[i], k_norm[i], ln_g[i], ln_b[i])
        y_sample = _layer(y_sample, w_in[i], w_out[i], q_norm[i], k_norm[i], ln_g[i], ln_b[i])
    return (y_prompt, y_sample)


_drawn_inputs = setup_inputs


def setup_inputs(seed=0):
    import zlib

    import numpy as np

    out = dict(_drawn_inputs(seed))
    spreads = {}
    factors = {'q_norm': 27.684, 'k_norm': 22.899, 'ln_g': 7.48, 'ln_b': 7.843}
    for name, (base, spread) in spreads.items():
        noise = np.random.default_rng([zlib.crc32(name.encode()), seed]).standard_normal(out[name].shape)
        drawn = base * np.exp(spread * noise) if base else spread * noise
        out[name] = __import__('jax').numpy.asarray(drawn.astype(out[name].dtype))
    for name, factor in factors.items():
        out[name] = (out[name] * factor).astype(out[name].dtype)
    return out
```

```python
import math
from contextlib import ExitStack

import numpy as np

import concourse.bass as bass
from concourse import mybir

F32 = mybir.dt.float32
F32R = mybir.dt.float32r
ALU = mybir.AluOpType
ACT = mybir.ActivationFunctionType
AX = mybir.AxisListType

P = 128
D_MODEL = 1024
SEQ, DEC_SEQ = 512, 256
HEAD_DIM = 64
N_HEADS_A, N_HEADS_B, N_KV_B = 8, 8, 2
WIDTH_A, WIDTH_B, KV_WIDTH = N_HEADS_A * HEAD_DIM, N_HEADS_B * HEAD_DIM, N_KV_B * HEAD_DIM
DILATED_PATTERNS = ((128, 1), (512, 4), (2048, 16))
GRID_W = 64
ROPE_THETA = 10000.0
LN_EPS, RMS_EPS = 1e-5, 1e-6
ALPHA = 2.0 ** 0.25
SCALE = HEAD_DIM ** -0.5
NEG_BIG = -1e30

QT = SEQ // P
ST = DEC_SEQ // P
TILES = QT + ST
TOK = TILES * P
KT = D_MODEL // P
CW = 256
HPC = CW // HEAD_DIM
COL = dict(qa=0, ka=WIDTH_A, va=2 * WIDTH_A, ga=3 * WIDTH_A, qb=4 * WIDTH_A,
           kb=4 * WIDTH_A + WIDTH_B, vb=4 * WIDTH_A + WIDTH_B + KV_WIDTH,
           gb=4 * WIDTH_A + WIDTH_B + 2 * KV_WIDTH)
IN_WIDTH = COL["gb"] + WIDTH_B
IN_CHUNKS, OUT_CHUNKS = IN_WIDTH // CW, D_MODEL // CW
CHUNKS = IN_CHUNKS + OUT_CHUNKS
ORDER = [8, 9, 10, 11, 12, 0, 1, 2, 3, 4, 5, 6, 7]
NORM, ROPE, VALUE, GATE = range(4)
KIND = {8: NORM, 9: NORM, 10: NORM, 11: GATE, 12: GATE, 0: ROPE, 1: ROPE, 2: ROPE, 3: ROPE,
        4: VALUE, 5: VALUE, 6: GATE, 7: GATE}

SLICES = KT // 2
RAW = 2
RING = 8
HEADS = N_HEADS_B + N_HEADS_A
UNITS = QT + 1
NU = HEADS * UNITS
PRING = 3

MASK_W = (QT - 1) * P + SEQ
C_IDENT, C_MASK = 0, P
C_COSA = C_MASK + MASK_W
C_SINA = C_COSA + QT * HEAD_DIM
C_COSB = C_SINA + QT * HEAD_DIM
C_SINB = C_COSB + QT * HEAD_DIM
C_W = C_SINB + QT * HEAD_DIM


def shape_constants():
    c = np.zeros((P, C_W), np.float32)
    c[:, C_IDENT:C_IDENT + P] = np.eye(P, dtype=np.float32)
    dist = np.arange(P)[:, None] - np.arange(MASK_W)[None, :] + (QT - 1) * P
    count = sum(((dist % dil == 0) & (abs(dist) <= dil * (window // (2 * dil)))).astype(np.int64)
                for window, dil in DILATED_PATTERNS)
    c[:, C_MASK:C_MASK + MASK_W] = np.where(count > 0, np.log(np.maximum(count, 1)) / SCALE, NEG_BIG)

    def angles(pos, dim):
        inv = 1.0 / (np.float32(ROPE_THETA) ** (np.arange(0, dim, 2, dtype=np.float32) / np.float32(dim)))
        a = pos.astype(np.float32)[:, None] * inv.astype(np.float32)[None, :]
        a = np.concatenate([a, a], -1)
        sign = np.where(np.arange(dim) < dim // 2, -1.0, 1.0)
        return np.cos(a), np.sin(a) * sign

    pos = np.arange(SEQ)
    cos_a, sin_a = angles(pos, HEAD_DIM)
    rows, cols = angles(pos // GRID_W, HEAD_DIM // 2), angles(pos % GRID_W, HEAD_DIM // 2)
    cos_b, sin_b = (np.concatenate([r, k], -1) for r, k in zip(rows, cols))
    for at, table in ((C_COSA, cos_a), (C_SINA, sin_a), (C_COSB, cos_b), (C_SINB, sin_b)):
        c[:, at:at + QT * HEAD_DIM] = table.reshape(QT, P, HEAD_DIM).transpose(1, 0, 2).reshape(P, -1)
    return c


def head_columns(j):
    if j < N_HEADS_B:
        kv = j // (N_HEADS_B // N_KV_B)
        return (COL["qb"] + 64 * j, COL["kb"] + 64 * kv, COL["vb"] + 64 * kv, COL["gb"] + 64 * j, kv, False)
    h = j - N_HEADS_B
    return (COL["qa"] + 64 * h, COL["ka"] + 64 * h, COL["va"] + 64 * h, COL["ga"] + 64 * h, N_KV_B + h, True)


def mix_batches_after():
    at = {}
    for j in range(1, HEADS, 2):
        e = j // 2 + (WIDTH_A // P if j < N_HEADS_B else -(N_HEADS_B // 2))
        at[j] = e
    return at


def build(nc, x_prompt, x_sample, w_in, w_out, q_norm, k_norm, ln_g, ln_b, consts, y_prompt, y_sample):
    ctx = ExitStack()
    with ctx:
        def sb(name, shape, dt=F32):
            return ctx.enter_context(nc.sbuf_tensor(name, shape, dt))

        def sem(name):
            return ctx.enter_context(nc.semaphore(name))

        t_hi = sb("t_hi", [P, KT, TOK], F32R)
        t_lo = sb("t_lo", [P, KT, TOK], F32R)
        w_hi = sb("w_hi", [P, RING, 2, CW], F32R)
        w_lo = sb("w_lo", [P, RING, 2, CW], F32R)
        q_st = sb("q_st", [P, 2, TOK], F32R)
        k_hi = sb("k_hi", [P, 2, TOK], F32R)
        k_lo = sb("k_lo", [P, 2, TOK], F32R)
        v_st = sb("v_st", [P, 2, TILES, 2 * HEAD_DIM], F32R)
        k_two = sb("k_two", [P, TILES, 2 * HEAD_DIM])
        p_hi = sb("p_hi", [P, 2, SEQ], F32R)
        p_lo = sb("p_lo", [P, 2, SEQ], F32R)
        h = sb("h", [P, TILES, IN_WIDTH])
        raw = sb("raw", [P, RAW, 2, CW])
        cst = sb("cst", [P, C_W])
        cosg = sb("cosg", [P, 2, QT, HEAD_DIM])
        sing = sb("sing", [P, 2, QT, HEAD_DIM])
        tmp_c = sb("tmp_c", [P, 2, CW])
        tmp_s = sb("tmp_s", [P, 2, CW])
        prob = sb("prob", [P, PRING, SEQ])
        tanh = prob[:, 0:2, 0:CW]
        nmax = sb("nmax", [P, HEADS, TILES])
        den = sb("den", [P, HEADS, TILES])
        rden = sb("rden", [P, HEADS, TILES])
        norms = sb("norms", [P, 2, HEAD_DIM])
        ssq = sb("ssq", [P, TILES, HPC])
        rstd = sb("rstd", [P, 2, TILES * HPC])
        stats = sb("stats", [P, TILES, OUT_CHUNKS, 6])
        mv = sb("mv", [P, TILES, 2])
        lnr = sb("lnr", [P, TILES, 4])
        half = sb("half", [P, TILES * HPC])
        zero = sb("zero", [P, 1])
        scr = sb("scr", [P, TILES * HPC])

        ident = cst[:, C_IDENT:C_IDENT + P]

        def table(at, t):
            k = t if t < QT else t - QT
            return cst[:, at + k * HEAD_DIM:at + (k + 1) * HEAD_DIM]

        bank = [ctx.enter_context(nc.psum_tensor(f"bank{i}", [P, 512], F32)) for i in range(8)]
        acc, s_ps, pt_ps, o_ps, t_ps = bank[0:2], bank[2:4], bank[4:6], bank[6], bank[7]

        x_loaded = [sem(f"x_loaded{t}") for t in range(TILES)]
        consts_loaded = sem("consts_loaded")
        norms_loaded = sem("norms_loaded")
        raw_loaded = [sem(f"raw_loaded{i}") for i in range(RAW)]
        hi_done = sem("w_hi_done")
        lo_done = sem("w_lo_done")
        tables_ready = sem("tables_ready")
        pool_consts = sem("pool_consts")
        xt_written, xt_hi, xt_lo = sem("xt_written"), sem("xt_hi"), sem("xt_lo")
        acc_ready = sem("acc_ready")
        act_evacuated, dve_evacuated = sem("act_evacuated"), sem("dve_evacuated")
        tanh_done = sem("tanh_done")
        products_ready, rope_added = sem("products_ready"), sem("rope_added")
        squared, summed, rstd_ready, normed = sem("squared"), sem("summed"), sem("rstd_ready"), sem("normed")
        pool_step, dve_step = sem("pool_step"), sem("dve_step")
        t_written, t_hi_done, t_lo_done = sem("t_written"), sem("t_hi_done"), sem("t_lo_done")
        v_split, keys_doubled = sem("v_split"), sem("keys_doubled")
        s_ready, s_masked = sem("s_ready"), sem("s_masked")
        exp_done = sem("exp_done")
        pt_ready, pt_hi_done, pt_lo_done = sem("pt_ready"), sem("pt_hi_done"), sem("pt_lo_done")
        pv_done = sem("pv_done")
        den_inverted, gate_scaled, mixed = sem("den_inverted"), sem("gate_scaled"), sem("mixed")
        xres_loaded = sem("xres_loaded")
        ln_loaded = sem("ln_loaded")
        stats_ready, ln_rstd, ln_normed, ln_scaled, y_ready = (
            sem("stats_ready"), sem("ln_rstd"), sem("ln_normed"), sem("ln_scaled"), sem("y_ready"))
        stored = sem("stored")

        block = ctx.enter_context(nc.Block())

        AHEAD = (IN_CHUNKS + 1) * SLICES + RAW
        IN_ITEMS = IN_CHUNKS * TILES
        evac = []
        n_act = n_dve = n_rot = 0
        for c in range(CHUNKS):
            kind = KIND[ORDER[c]] if c < IN_CHUNKS else None
            by_act = kind in (NORM, VALUE)
            for t in range(TILES):
                n_rot += kind in (NORM, ROPE)
                if by_act:
                    n_act += 1
                    evac.append((act_evacuated, n_act))
                elif kind == ROPE:
                    evac.append((products_ready, n_rot))
                else:
                    n_dve += 1
                    evac.append((dve_evacuated, n_dve))
        gates = [(c, t) for c in range(IN_CHUNKS) if KIND[ORDER[c]] == GATE for t in range(TILES)]
        gate_evac = [evac[c * TILES + t][1] for c, t in gates]

        def i_gate(c, t):
            return gates.index((c, t))

        ropes = []
        for c in range(IN_CHUNKS):
            if KIND[ORDER[c]] in (NORM, ROPE):
                ropes += [(c, t) for t in range(TILES)]

        def chunk_source(c):
            if c < IN_CHUNKS:
                w, at = w_in, ORDER[c] * CW
            else:
                w, at = w_out, (c - IN_CHUNKS) * CW
            return w[:, at:at + CW].rearrange("(k p) n -> p k n", p=P)

        def x_rows(t):
            return x_prompt[t * P:(t + 1) * P, :] if t < QT else x_sample[(t - QT) * P:(t - QT + 1) * P, :]

        def y_rows(t):
            return y_prompt[t * P:(t + 1) * P, :] if t < QT else y_sample[(t - QT) * P:(t - QT + 1) * P, :]

        own_kv = [j == 0 or head_columns(j)[4] != head_columns(j - 1)[4] for j in range(HEADS)]

        def staging(j):
            return [("q", j)] + ([("k", j)] if own_kv[j] else []) + [("r", j)]

        mixes = mix_batches_after()
        steps = {u: [] for u in range(NU + 3)}
        for j in range(HEADS - 1):
            for n, b in enumerate(staging(j + 1)):
                steps[UNITS * j + (0, 2, 3)[n]].append(b)
        for j in range(1, HEADS - 2, 2):
            e = mixes[j]
            steps[UNITS * (j + 1) + 4].append(("m", e, 0, QT, j))
            steps[UNITS * (j + 2) + 1].append(("m", e, QT, ST, j))
        first = staging(0)
        last = [("m", mixes[HEADS - 1], 0, QT, HEADS - 1), ("m", mixes[HEADS - 1], QT, ST, HEADS - 1)]
        t_count = {}
        for b in first + [b for u in range(NU + 3) for b in steps[u]] + last:
            t_count[b] = len(t_count)
        staged = [t_count[staging(j)[-1]] + 1 for j in range(HEADS)]

        @block.sync
        def _(sp):
            def load_slice(g):
                if g >= RAW:
                    sp.wait_ge(lo_done, g - RAW + 1)
                c, s = divmod(g, SLICES)
                sp.dma_start(raw[:, g % RAW, :, :], chunk_source(c)[:, 2 * s:2 * s + 2, :]) \
                    .then_inc(raw_loaded[g % RAW], 16)

            for t in range(TILES):
                sp.dma_start(h[:, t, 0:D_MODEL], x_rows(t)).then_inc(x_loaded[t], 16)
                if t < RAW:
                    load_slice(t)
            for g in range(RAW, AHEAD):
                load_slice(g)
            sp.wait_ge(t_written, staged[HEADS - 1])
            sp.wait_ge(v_split, HEADS // 2 + N_KV_B)
            for t in range(TILES):
                sp.dma_start(h[:, t, 0:D_MODEL], x_rows(t)).then_inc(xres_loaded, 16)
            for n, src in enumerate((ln_g, ln_b)):
                for k in range(2):
                    sp.dma_start(h[:, 2 * n + k, 2 * WIDTH_A:3 * WIDTH_A],
                                 src[None, k * 512:(k + 1) * 512].to_broadcast([P, 512])).then_inc(ln_loaded, 16)
            for g in range(AHEAD, CHUNKS * SLICES):
                load_slice(g)
            for t in range(TILES):
                sp.wait_ge(y_ready, t + 1)
                sp.dma_start(y_rows(t), h[:, t, 0:D_MODEL]).then_inc(stored, 16)
            sp.wait_ge(stored, 16 * TILES)

        @block.tensor
        def _(pe):
            def transpose_batch(dst, pieces):
                for n, src in enumerate(pieces):
                    ins = nc.tensor.transpose(dst[0:src.shape[-1], n * P:(n + 1) * P], src, ident)
                return ins

            def x_transposes(t):
                pe.wait_ge(x_loaded[t], 16)
                for b in range(2):
                    i = 2 * t + b
                    if i >= 2:
                        pe.wait_ge(xt_lo, i - 1)
                    transpose_batch(pt_ps[i % 2], [h[:, t, (4 * b + n) * P:(4 * b + n + 1) * P] for n in range(4)]) \
                        .then_inc(xt_written, 1)

            def project(c, t):
                i = c * TILES + t
                if i >= 2:
                    pe.wait_ge(*evac[i - 2])
                out = acc[i % 2][:, 0:CW]
                for k in range(KT):
                    g = c * SLICES + k // 2
                    if t == 0 and k % 2 == 0:
                        pe.wait_ge(lo_done, g + 1)
                    a_hi, a_lo = t_hi[:, k, t * P:(t + 1) * P], t_lo[:, k, t * P:(t + 1) * P]
                    b_hi, b_lo = w_hi[:, g % RING, k % 2, :], w_lo[:, g % RING, k % 2, :]
                    nc.tensor.matmul(out, a_lo, b_hi, start=(k == 0), stop=False)
                    nc.tensor.matmul(out, a_hi, b_lo, start=False, stop=False)
                    ins = nc.tensor.matmul(out, a_hi, b_hi, start=False, stop=(k == KT - 1))
                ins.then_inc(acc_ready, 1)

            def t_batch(b):
                n = t_count[b]
                if n:
                    pe.wait_ge(t_lo_done, n)
                if b[0] == "m":
                    _, e, t0, nt, j = b
                    pe.wait_ge(mixed, j + 1)
                    at = COL["ga"] + e * P if e < WIDTH_A // P else COL["gb"] + e * P - WIDTH_A
                    pieces = [h[:, t0 + t, at:at + P] for t in range(nt)]
                else:
                    qc, kc = head_columns(b[1])[0:2]
                    if b[0] == "q":
                        pieces = [h[:, t, qc:qc + HEAD_DIM] for t in range(QT)]
                    elif b[0] == "k":
                        pe.wait_ge(keys_doubled, head_columns(b[1])[4] + 1)
                        pieces = [k_two[:, t, :] for t in range(QT)]
                    else:
                        pieces = [h[:, QT + t, qc:qc + HEAD_DIM] for t in range(ST)]
                        if own_kv[b[1]]:
                            pieces += [k_two[:, QT + t, :] for t in range(ST)]
                transpose_batch(t_ps, pieces).then_inc(t_written, 1)

            def scores(u):
                j, k = divmod(u, UNITS)
                kv = head_columns(j)[4]
                if k == 0:
                    pe.wait_ge(t_lo_done, staged[j])
                if u >= 2:
                    pe.wait_ge(s_masked, u - 1)
                out = s_ps[u % 2]
                q = q_st[:, j % 2, :]
                if k < QT:
                    nc.tensor.matmul(out[:], q[:, k * P:(k + 1) * P], k_lo[:, kv % 2, 0:SEQ], start=True, stop=False)
                    ins = nc.tensor.matmul(out[:], q[:, k * P:(k + 1) * P], k_hi[:, kv % 2, 0:SEQ],
                                           start=False, stop=True)
                else:
                    for t in range(ST):
                        o = out[:, t * DEC_SEQ:(t + 1) * DEC_SEQ]
                        lhs = q[:, SEQ + t * P:SEQ + (t + 1) * P]
                        nc.tensor.matmul(o, lhs, k_lo[:, kv % 2, SEQ:TOK], start=True, stop=False)
                        ins = nc.tensor.matmul(o, lhs, k_hi[:, kv % 2, SEQ:TOK], start=False, stop=True)
                ins.then_inc(s_ready, 1)

            def prob_transposes(u):
                pe.wait_ge(exp_done, u + 1)
                if u >= 2:
                    pe.wait_ge(pt_lo_done, u - 1)
                transpose_batch(pt_ps[u % 2], [prob[:, u % PRING, n * P:(n + 1) * P] for n in range(4)]) \
                    .then_inc(pt_ready, 1)

            def values(u):
                j, k = divmod(u, UNITS)
                kv = head_columns(j)[4]
                if k == 0:
                    pe.wait_ge(v_split, kv + 1)
                    if j:
                        pe.wait_ge(mixed, j)
                pe.wait_ge(pt_lo_done, u + 1)
                groups = [(k, range(QT), 0)] if k < QT else [(QT + t, range(ST), t * ST) for t in range(ST)]
                for t, keys, first_piece in groups:
                    o = o_ps[:, t * HEAD_DIM:(t + 1) * HEAD_DIM]
                    base = 0 if k < QT else QT
                    for n in keys:
                        at = (first_piece + n) * P
                        vh = v_st[:, kv % 2, base + n, 0:HEAD_DIM]
                        vl = v_st[:, kv % 2, base + n, HEAD_DIM:2 * HEAD_DIM]
                        nc.tensor.matmul(o, p_lo[:, u % 2, at:at + P], vh, start=(n == 0), stop=False)
                        nc.tensor.matmul(o, p_hi[:, u % 2, at:at + P], vl, start=False, stop=False)
                        ins = nc.tensor.matmul(o, p_hi[:, u % 2, at:at + P], vh,
                                               start=False, stop=(n == len(keys) - 1))
                ins.then_inc(pv_done, 1)

            pe.wait_ge(consts_loaded, 16)
            x_transposes(0)
            for t in range(TILES):
                if t + 1 < TILES:
                    x_transposes(t + 1)
                pe.wait_ge(xt_lo, 2 * t + 2)
                project(0, t)
            for c in range(1, IN_CHUNKS):
                for t in range(TILES):
                    project(c, t)
            pe.wait_ge(rope_added, (7 * TILES))
            pe.wait_ge(act_evacuated, n_act)
            for b in first:
                t_batch(b)
            for u in range(NU + 3):
                if u < NU:
                    scores(u)
                for b in steps[u]:
                    t_batch(b)
                if 2 <= u < NU + 2:
                    prob_transposes(u - 2)
                if u >= 3:
                    values(u - 3)
            for b in last:
                t_batch(b)
            pe.wait_ge(t_lo_done, len(t_count))
            for c in range(IN_CHUNKS, CHUNKS):
                for t in range(TILES):
                    project(c, t)

        def t_destination(b):
            if b[0] == "m":
                _, e, t0, nt, j = b
                return [(0, nt * P, t_hi[:, e, t0 * P:(t0 + nt) * P])]
            j = b[1]
            kv = head_columns(j)[4]
            if b[0] == "q":
                return [(0, SEQ, q_st[0:HEAD_DIM, j % 2, 0:SEQ])]
            if b[0] == "k":
                return [(0, SEQ, k_hi[:, kv % 2, 0:SEQ])]
            out = [(0, DEC_SEQ, q_st[0:HEAD_DIM, j % 2, SEQ:TOK])]
            if own_kv[j]:
                out.append((DEC_SEQ, 2 * DEC_SEQ, k_hi[:, kv % 2, SEQ:TOK]))
            return out

        @block.scalar
        def _(act):
            act.dma_start(cst[:], consts[:, :]).then_inc(consts_loaded, 16)
            act.dma_start(norms[:, 0, :], q_norm[None, :].to_broadcast([P, HEAD_DIM])).then_inc(norms_loaded, 16)
            act.dma_start(norms[:, 1, :], k_norm[None, :].to_broadcast([P, HEAD_DIM])).then_inc(norms_loaded, 16)

            def weights_high(g):
                act.wait_ge(raw_loaded[g % RAW], 16 * (g // RAW + 1))
                if g >= RING:
                    act.wait_ge(acc_ready, TILES * (g // SLICES - RING // SLICES + 1))
                nc.scalar.activation(w_hi[:, g % RING, :, :], raw[:, g % RAW, :, :], ACT.Copy).then_inc(hi_done, 1)

            def x_high(t):
                for b in range(2):
                    i = 2 * t + b
                    act.wait_ge(xt_written, i + 1)
                    nc.scalar.activation(t_hi[:, 4 * b:4 * b + 4, t * P:(t + 1) * P],
                                         pt_ps[i % 2][:].rearrange("p (n q) -> p n q", n=4), ACT.Copy) \
                        .then_inc(xt_hi, 1)

            def evacuate(c, t):
                i = c * TILES + t
                kind = KIND[ORDER[c]]
                if kind == ROPE:
                    return
                act.wait_ge(acc_ready, i + 1)
                at = ORDER[c] * CW
                if kind == GATE:
                    n = i_gate(c, t)
                    if n >= 2:
                        act.wait_ge(dve_evacuated, gate_evac[n - 2])
                    nc.scalar.activation(tanh[:, n % 2, :], acc[i % 2][:, 0:CW], ACT.Tanh, scale=0.5) \
                        .then_inc(tanh_done, 1)
                else:
                    nc.scalar.activation(h[:, t, at:at + CW], acc[i % 2][:, 0:CW], ACT.Copy).then_inc(act_evacuated, 1)

            def t_high(b):
                n = t_count[b]
                act.wait_ge(t_written, n + 1)
                if b[0] in ("q", "k"):
                    j = b[1]
                    if j >= 2:
                        act.wait_ge(s_ready, UNITS * (j - 1))
                for a, z, dst in t_destination(b):
                    ins = nc.scalar.activation(dst, t_ps[0:dst.shape[0], a:z], ACT.Copy)
                ins.then_inc(t_hi_done, 1)

            def exps(u):
                j, k = divmod(u, UNITS)
                act.wait_ge(s_masked, u + 1)
                rows = [(k, 0, SEQ)] if k < QT else [(QT + t, t * DEC_SEQ, (t + 1) * DEC_SEQ) for t in range(ST)]
                for t, a, z in rows:
                    s = prob[:, u % PRING, a:z]
                    ins = nc.scalar.activation(s, s, ACT.Exp, scale=-1.0, bias=nmax[:, j, t:t + 1],
                                               accum_out=den[:, j, t:t + 1])
                ins.then_inc(exp_done, 1)

            def prob_high(u):
                act.wait_ge(pt_ready, u + 1)
                if u >= 2:
                    act.wait_ge(pv_done, u - 1)
                nc.scalar.activation(p_hi[:, u % 2, :], pt_ps[u % 2][:], ACT.Copy).then_inc(pt_hi_done, 1)

            for g in range(2):
                weights_high(g)
            x_high(0)
            for g in range(2, 4):
                weights_high(g)
            for t in range(1, TILES):
                x_high(t)
                evacuate(0, t - 1)
                if t < 5:
                    weights_high(SLICES + t - 1)
            evacuate(0, TILES - 1)
            for c in range(1, IN_CHUNKS):
                for t in range(TILES):
                    if 1 <= t < 5:
                        weights_high((c + 1) * SLICES + t - 1)
                    evacuate(c, t)
            for b in first:
                t_high(b)
            for u in range(NU + 2):
                for b in steps[u]:
                    t_high(b)
                if u >= 2:
                    prob_high(u - 2)
                if u < NU:
                    exps(u)
            for b in last:
                t_high(b)
            for c in range(IN_CHUNKS, CHUNKS):
                for s in range(SLICES):
                    if c + 1 < CHUNKS:
                        weights_high((c + 1) * SLICES + s)
            for t in range(TILES):
                act.wait_ge(ln_rstd, t + 1)
                r = h[:, t, 0:D_MODEL]
                nc.scalar.activation(r, r, ACT.Identity, scale=lnr[:, t, 0:1], bias=lnr[:, t, 1:2]) \
                    .then_inc(ln_normed, 1)

        @block.vector
        def _(dve):
            links = [0]

            def after(ins):
                links[0] += 1
                ins.then_inc(dve_step, 1)
                dve.wait_ge(dve_step, links[0])

            def swap_halves(out, in_, tab, heads, block_w):
                n = HEAD_DIM // block_w
                w = block_w // 2
                for a, b in ((0, w), (w, 0)):
                    for k in range(n):
                        o = out.rearrange("p (m d) -> p m d", d=HEAD_DIM)[:, :, k * block_w + a:k * block_w + a + w]
                        i = in_.rearrange("p (m d) -> p m d", d=HEAD_DIM)[:, :, k * block_w + b:k * block_w + b + w]
                        tt = tab[:, None, k * block_w + a:k * block_w + a + w].to_broadcast([P, heads, w])
                        ins = nc.vector.tensor_tensor(o, i, tt, ALU.mult)
                return ins

            def heads_of(ap):
                return ap.rearrange("p (m d) -> p m d", d=HEAD_DIM)

            def x_low(t):
                for b in range(2):
                    i = 2 * t + b
                    dve.wait_ge(xt_hi, i + 1)
                    at = t_hi[:, 4 * b:4 * b + 4, t * P:(t + 1) * P]
                    nc.vector.tensor_tensor(t_lo[:, 4 * b:4 * b + 4, t * P:(t + 1) * P],
                                            pt_ps[i % 2][:].rearrange("p (n q) -> p n q", n=4),
                                            at.bitcast(F32), ALU.subtract).then_inc(xt_lo, 1)

            def rotate(src, cos, sin, heads, block_w, n):
                if n >= 2:
                    dve.wait_ge(rope_added, n - 1)
                nc.vector.tensor_tensor(heads_of(tmp_c[:, n % 2, 0:heads * HEAD_DIM]), heads_of(src),
                                        cos[:, None, :].to_broadcast([P, heads, HEAD_DIM]), ALU.mult)
                ins = swap_halves(tmp_s[:, n % 2, 0:heads * HEAD_DIM], src, sin, heads, block_w)
                ins.then_inc(products_ready, 1)

            def norm_heads(c):
                return N_KV_B if ORDER[c] == 10 else HPC

            def sums(c, t):
                n = c * TILES + t
                dve.wait_ge(squared, n + 1)
                m = norm_heads(c)
                nc.vector.reduce_sum(ssq[:, t, 0:m], heads_of(tmp_s[:, n % 2, 0:m * HEAD_DIM]), axis=AX.X) \
                    .then_inc(summed, 1)

            def norm_and_rotate(c):
                which = 1 if ORDER[c] == 10 else 0
                m = norm_heads(c)
                dve.wait_ge(rstd_ready, c + 1)
                for t in range(TILES):
                    n = c * TILES + t
                    src = h[:, t, ORDER[c] * CW:ORDER[c] * CW + m * HEAD_DIM]
                    k = t if t < QT else t - QT
                    r = rstd[:, c % 2, t * HPC:t * HPC + m]
                    after(nc.vector.tensor_tensor(heads_of(src), heads_of(src),
                                                  r[:, :, None].to_broadcast([P, m, HEAD_DIM]), ALU.mult))
                    rotate(src, cosg[:, which, k, :], sing[:, which, k, :], m, HEAD_DIM // 2, n)

            def mask_max(u):
                j, k = divmod(u, UNITS)
                is_a = head_columns(j)[5]
                dve.wait_ge(s_ready, u + 1)
                if u >= PRING:
                    dve.wait_ge(pt_ready, u - PRING + 1)
                rows = [(k, 0, SEQ)] if k < QT else [(QT + t, t * DEC_SEQ, (t + 1) * DEC_SEQ) for t in range(ST)]
                for t, a, z in rows:
                    if is_a:
                        m0 = C_MASK + (QT - 1 - (t if t < QT else t - QT)) * P
                        mask = cst[:, m0:m0 + z - a]
                    else:
                        mask = zero[:].to_broadcast([P, z - a])
                    ins = nc.vector.tensor_tensor_reduce(
                        out=prob[:, u % PRING, a:z], in0=s_ps[u % 2][:, a:z], in1=mask, scale=-SCALE,
                        scalar=-NEG_BIG, op0=ALU.add, op1=ALU.min, accum_out=nmax[:, j, t:t + 1])
                ins.then_inc(s_masked, 1)

            def prob_low(u):
                dve.wait_ge(pt_hi_done, u + 1)
                nc.vector.tensor_tensor(p_lo[:, u % 2, :], pt_ps[u % 2][:], p_hi[:, u % 2, :].bitcast(F32),
                                        ALU.subtract).then_inc(pt_lo_done, 1)

            def t_low(b):
                n = t_count[b]
                dve.wait_ge(t_hi_done, n + 1)
                for a, z, dst in t_destination(b):
                    if b[0] == "m":
                        _, e, t0, nt, j = b
                        ins = nc.vector.tensor_tensor(t_lo[:, e, t0 * P:(t0 + nt) * P], t_ps[:, a:z],
                                                      dst.bitcast(F32), ALU.subtract)
                    elif b[0] == "k" or a:
                        kv = head_columns(b[1])[4]
                        lo = k_lo[:, kv % 2, 0:SEQ] if b[0] == "k" else k_lo[:, kv % 2, SEQ:TOK]
                        ins = nc.vector.tensor_tensor(lo, t_ps[:, a:z], dst.bitcast(F32), ALU.subtract)
                    else:
                        low = q_st[HEAD_DIM:P, b[1] % 2, 0:SEQ] if b[0] == "q" else \
                            q_st[HEAD_DIM:P, b[1] % 2, SEQ:TOK]
                        ins = nc.vector.tensor_tensor(low, t_ps[0:HEAD_DIM, a:z], dst.bitcast(F32), ALU.subtract)
                ins.then_inc(t_lo_done, 1)

            def invert(j):
                dve.wait_ge(exp_done, UNITS * (j + 1))
                nc.vector.reciprocal(rden[:, j, :], den[:, j, :]).then_inc(den_inverted, 1)

            def mix(j):
                dve.wait_ge(gate_scaled, j + 1)
                dve.wait_ge(pv_done, UNITS * (j + 1))
                g0 = head_columns(j)[3]
                g = h[:, :, g0:g0 + HEAD_DIM]
                nc.vector.scalar_tensor_tensor(
                    out=g, in0=o_ps[:, 0:TILES * HEAD_DIM].rearrange("p (t d) -> p t d", d=HEAD_DIM),
                    scalar=0.5, in1=g, op0=ALU.mult, op1=ALU.mult).then_inc(mixed, 1)

            nc.vector.memset(zero[:], 0.0)
            nc.vector.memset(half[:], -0.5).then_inc(pool_consts, 1)
            dve.wait_ge(consts_loaded, 16)
            dve.wait_ge(norms_loaded, 32)
            for w in range(2):
                g = norms[:, w, :]
                nc.vector.tensor_tensor(cosg[:, w], cst[:, C_COSB:C_COSB + QT * HEAD_DIM]
                                        .rearrange("p (t d) -> p t d", d=HEAD_DIM),
                                        g[:, None, :].to_broadcast([P, QT, HEAD_DIM]), ALU.mult)
                sin = cst[:, C_SINB:C_SINB + QT * HEAD_DIM].rearrange("p (t d) -> p t d", d=HEAD_DIM)
                q = HEAD_DIM // 4
                for k in range(4):
                    o = k ^ 1
                    nc.vector.tensor_tensor(sing[:, w, :, k * q:(k + 1) * q], sin[:, :, k * q:(k + 1) * q],
                                            g[:, None, o * q:(o + 1) * q].to_broadcast([P, QT, q]), ALU.mult) \
                        .then_inc(tables_ready, 1)
            dve.wait_ge(tables_ready, 8)
            x_low(0)
            for t in range(1, TILES):
                x_low(t)
                sums(0, t - 1)
            sums(0, TILES - 1)
            norm_and_rotate(0)
            for c in (1, 2):
                for t in range(TILES):
                    sums(c, t)
                norm_and_rotate(c)
            for c in range(3, IN_CHUNKS):
                kind = KIND[ORDER[c]]
                for t in range(TILES):
                    i = c * TILES + t
                    k = t if t < QT else t - QT
                    if kind == GATE:
                        n = i_gate(c, t)
                        dve.wait_ge(tanh_done, n + 1)
                        nc.vector.scalar_tensor_tensor(
                            out=h[:, t, ORDER[c] * CW:(ORDER[c] + 1) * CW], in0=tanh[:, n % 2, :], scalar=1.0,
                            in1=acc[i % 2][:, 0:CW], op0=ALU.add, op1=ALU.mult).then_inc(dve_evacuated, 1)
                    elif kind == ROPE:
                        n = ropes.index((c, t))
                        dve.wait_ge(acc_ready, i + 1)
                        rotate(acc[i % 2][:, 0:CW], table(C_COSA, t), table(C_SINA, t), HPC, HEAD_DIM, n)
            for b in first:
                t_low(b)
            for u in range(NU + 3):
                if u < NU:
                    mask_max(u)
                for b in steps[u]:
                    t_low(b)
                if 2 <= u < NU + 2:
                    prob_low(u - 2)
                j, k = divmod(u, UNITS)
                if k == 1 and j:
                    invert(j - 1)
                if k == 3 and j:
                    mix(j - 1)
            mix(HEADS - 1)
            for b in last:
                t_low(b)
            for c in range(OUT_CHUNKS):
                for t in range(TILES):
                    i = (IN_CHUNKS + c) * TILES + t
                    r = h[:, t, c * CW:(c + 1) * CW]
                    dve.wait_ge(acc_ready, i + 1)
                    if c == 0 and t == 0:
                        dve.wait_ge(xres_loaded, 16 * TILES)
                    after(nc.vector.scalar_tensor_tensor(out=r, in0=r, scalar=ALPHA, in1=acc[i % 2][:, 0:CW],
                                                         op0=ALU.mult, op1=ALU.add))
                    last_i = nc.vector.bn_stats(stats[:, t, c, :], r)
                    last_i.then_inc(dve_evacuated, 1)
                    if c == OUT_CHUNKS - 1:
                        dve.wait_ge(dve_evacuated, evac[i][1])
                        nc.vector.bn_aggr(mv[:, t, :], stats[:, t, :, :]).then_inc(stats_ready, 1)
            dve.wait_ge(ln_loaded, 64)
            for t in range(TILES):
                dve.wait_ge(ln_normed, t + 1)
                for k in range(2):
                    r = h[:, t, k * 512:(k + 1) * 512]
                    after(nc.vector.tensor_tensor(r, r, h[:, k, 2 * WIDTH_A:3 * WIDTH_A], ALU.mult))
                    ins = nc.vector.tensor_tensor(r, r, h[:, 2 + k, 2 * WIDTH_A:3 * WIDTH_A], ALU.add)
                ins.then_inc(y_ready, 1)

        @block.gpsimd
        def _(pool):
            links = [0]

            def after(ins):
                links[0] += 1
                ins.then_inc(pool_step, 1)
                pool.wait_ge(pool_step, links[0])

            def inverse_root(out, v, y, n):
                after(nc.gpsimd.tensor_tensor(y, v, half[:, 0:n], ALU.pow))
                after(nc.gpsimd.tensor_tensor(out, y, y, ALU.mult))
                after(nc.gpsimd.tensor_tensor(out, out, v, ALU.mult))
                after(nc.gpsimd.tensor_scalar(out, out, -0.5, 1.5, ALU.mult, ALU.add))
                return nc.gpsimd.tensor_tensor(out, out, y, ALU.mult)

            def weights_low(g):
                pool.wait_ge(hi_done, g + 1)
                nc.gpsimd.tensor_tensor(w_lo[:, g % RING, :, :], raw[:, g % RAW, :, :],
                                        w_hi[:, g % RING, :, :].bitcast(F32), ALU.subtract).then_inc(lo_done, 1)

            def square(c, t):
                n = c * TILES + t
                m = N_KV_B if ORDER[c] == 10 else HPC
                pool.wait_ge(act_evacuated, n + 1)
                if n >= 2:
                    pool.wait_ge(summed, n - 1)
                if t < 2 and c:
                    pool.wait_ge(rope_added, c * TILES)
                src = h[:, t, ORDER[c] * CW:ORDER[c] * CW + m * HEAD_DIM]
                nc.gpsimd.tensor_tensor(tmp_s[:, n % 2, 0:m * HEAD_DIM], src, src, ALU.mult).then_inc(squared, 1)

            def head_rstd(c):
                m = N_KV_B if ORDER[c] == 10 else HPC
                pool.wait_ge(summed, (c + 1) * TILES)
                v = ssq[:].rearrange("p t m -> p (t m)")
                if m == HPC:
                    n = TILES * HPC
                    out, y = rstd[:, c % 2, :], scr[:, 0:n]
                    after(nc.gpsimd.tensor_scalar(v, v, 1.0 / HEAD_DIM, RMS_EPS, ALU.mult, ALU.add))
                    inverse_root(out, v, y, n).then_inc(rstd_ready, 1)
                else:
                    vk = ssq[:, :, 0:m]
                    out = rstd[:, c % 2, :].rearrange("p (t m) -> p t m", m=HPC)[:, :, 0:m]
                    y = scr[:].rearrange("p (t m) -> p t m", m=HPC)[:, :, 0:m]
                    hf = half[:].rearrange("p (t m) -> p t m", m=HPC)[:, :, 0:m]
                    after(nc.gpsimd.tensor_scalar(vk, vk, 1.0 / HEAD_DIM, RMS_EPS, ALU.mult, ALU.add))
                    after(nc.gpsimd.tensor_tensor(y, vk, hf, ALU.pow))
                    after(nc.gpsimd.tensor_tensor(out, y, y, ALU.mult))
                    after(nc.gpsimd.tensor_tensor(out, out, vk, ALU.mult))
                    after(nc.gpsimd.tensor_scalar(out, out, -0.5, 1.5, ALU.mult, ALU.add))
                    nc.gpsimd.tensor_tensor(out, out, y, ALU.mult).then_inc(rstd_ready, 1)

            def add_rotation(c, t):
                n = ropes.index((c, t))
                m = N_KV_B if ORDER[c] == 10 else HPC
                pool.wait_ge(products_ready, n + 1)
                if ORDER[c] < 4:
                    pool.wait_ge(xt_written, 2 * TILES)
                nc.gpsimd.tensor_tensor(h[:, t, ORDER[c] * CW:ORDER[c] * CW + m * HEAD_DIM],
                                        tmp_c[:, n % 2, 0:m * HEAD_DIM], tmp_s[:, n % 2, 0:m * HEAD_DIM],
                                        ALU.add).then_inc(rope_added, 1)

            def split_values(j):
                _, _, vc, _, kv, _ = head_columns(j)
                if kv >= 2:
                    pool.wait_ge(pv_done, UNITS * (N_HEADS_B // N_KV_B * (kv - 1) if kv <= N_KV_B else
                                                   N_HEADS_B + kv - 1 - N_KV_B))
                hi = v_st[:, kv % 2, :, 0:HEAD_DIM]
                src = h[:, :, vc:vc + HEAD_DIM]
                after(nc.gpsimd.tensor_scalar(hi, src, 1.0, 0.0, ALU.mult, ALU.add))
                nc.gpsimd.tensor_tensor(v_st[:, kv % 2, :, HEAD_DIM:2 * HEAD_DIM], src, hi.bitcast(F32),
                                        ALU.subtract).then_inc(v_split, 1)

            def double_keys(j):
                kc, kv = head_columns(j)[1], head_columns(j)[4]
                if kv:
                    before = max(i for i in range(j) if own_kv[i])
                    pool.wait_ge(t_written, t_count[("r", before)] + 1)
                out = k_two[:].rearrange("p t (n d) -> p t n d", n=2)
                nc.gpsimd.tensor_scalar(out, h[:, :, None, kc:kc + HEAD_DIM].to_broadcast([P, TILES, 2, HEAD_DIM]),
                                        1.0, 0.0, ALU.mult, ALU.add).then_inc(keys_doubled, 1)

            def scale_gate(j):
                pool.wait_ge(den_inverted, j + 1)
                g0 = head_columns(j)[3]
                g = h[:, :, g0:g0 + HEAD_DIM]
                nc.gpsimd.tensor_tensor(g, g, rden[:, j, :, None].to_broadcast([P, TILES, HEAD_DIM]), ALU.mult) \
                    .then_inc(gate_scaled, 1)

            pool.wait_ge(pool_consts, 1)
            for g in range(4):
                weights_low(g)
            for t in range(TILES):
                square(0, t)
                if 1 <= t < 5:
                    weights_low(SLICES + t - 1)
            head_rstd(0)
            for t in range(TILES):
                add_rotation(0, t)
            for c in range(1, IN_CHUNKS):
                kind = KIND[ORDER[c]]
                for t in range(TILES):
                    if 1 <= t < 5:
                        weights_low((c + 1) * SLICES + t - 1)
                    if kind == NORM:
                        square(c, t)
                    elif kind == ROPE:
                        add_rotation(c, t)
                if kind == NORM:
                    head_rstd(c)
                    for t in range(TILES):
                        add_rotation(c, t)
            pool.wait_ge(act_evacuated, n_act)
            pool.wait_ge(dve_evacuated, evac[IN_ITEMS - 1][1])
            double_keys(0)
            split_values(0)
            for j in range(HEADS):
                ahead = j + 1 < HEADS and own_kv[j + 1]
                if ahead:
                    double_keys(j + 1)
                if j:
                    scale_gate(j - 1)
                if ahead:
                    split_values(j + 1)
            scale_gate(HEADS - 1)
            for g in range((IN_CHUNKS + 1) * SLICES, CHUNKS * SLICES):
                weights_low(g)
            for t in range(TILES):
                pool.wait_ge(stats_ready, t + 1)
                v, m = mv[:, t, 1:2], mv[:, t, 0:1]
                after(nc.gpsimd.tensor_scalar(lnr[:, t, 2:3], v, 1.0, LN_EPS, ALU.mult, ALU.add))
                after(inverse_root(lnr[:, t, 0:1], lnr[:, t, 2:3], lnr[:, t, 3:4], 1))
                after(nc.gpsimd.tensor_tensor(lnr[:, t, 1:2], lnr[:, t, 0:1], m, ALU.mult))
                nc.gpsimd.tensor_scalar(lnr[:, t, 1:2], lnr[:, t, 1:2], -1.0, 0.0, ALU.mult, ALU.add) \
                    .then_inc(ln_rstd, 1)


def kernel(**inputs):
    import concourse.bacc as bacc
    from concourse.bass_utils import run_bass_kernel_spmd

    nc = bacc.Bacc("TRN2", target_bir_lowering=False, num_devices=1, dynamic_dma_scratch_size=1024)
    arrays = {
        "x_prompt": np.ascontiguousarray(inputs["x_prompt"][0]),
        "x_sample": np.ascontiguousarray(inputs["x_sample"][0]),
        "w_in": np.ascontiguousarray(inputs["w_in"][0]),
        "w_out": np.ascontiguousarray(inputs["w_out"][0]),
        "q_norm": np.ascontiguousarray(inputs["q_norm"][0]),
        "k_norm": np.ascontiguousarray(inputs["k_norm"][0]),
        "ln_g": np.ascontiguousarray(inputs["ln_g"][0]),
        "ln_b": np.ascontiguousarray(inputs["ln_b"][0]),
        "consts": shape_constants(),
    }
    args = [nc.dram_tensor(n, a.shape, F32, kind="ExternalInput").ap() for n, a in arrays.items()]
    args += [nc.dram_tensor(n, (s, D_MODEL), F32, kind="ExternalOutput").ap()
             for n, s in (("y_prompt", SEQ), ("y_sample", DEC_SEQ))]
    build(nc, *args)
    r = run_bass_kernel_spmd(nc, [arrays], core_ids=[0])
    return (r.results[0]["y_prompt"].reshape(1, SEQ, D_MODEL), r.results[0]["y_sample"].reshape(1, DEC_SEQ, D_MODEL))
```

```python
import math
from contextlib import ExitStack

import numpy as np

import concourse.bass as bass
from concourse import mybir

F32 = mybir.dt.float32
F32R = mybir.dt.float32r
ALU = mybir.AluOpType
ACT = mybir.ActivationFunctionType
AX = mybir.AxisListType

P = 128
D_MODEL = 1024
SEQ, DEC_SEQ = 512, 256
HEAD_DIM = 64
N_HEADS_A, N_HEADS_B, N_KV_B = 8, 8, 2
WIDTH_A, WIDTH_B, KV_WIDTH = N_HEADS_A * HEAD_DIM, N_HEADS_B * HEAD_DIM, N_KV_B * HEAD_DIM
DILATED_PATTERNS = ((128, 1), (512, 4), (2048, 16))
GRID_W = 64
ROPE_THETA = 10000.0
LN_EPS, RMS_EPS = 1e-5, 1e-6
ALPHA = 2.0 ** 0.25
SCALE = HEAD_DIM ** -0.5
NEG_BIG = -1e30

QT = SEQ // P
ST = DEC_SEQ // P
TILES = QT + ST
TOK = TILES * P
KT = D_MODEL // P
CW = 256
HPC = CW // HEAD_DIM
IN_WIDTH = 4 * WIDTH_A + 2 * WIDTH_B + 2 * KV_WIDTH
IN_CHUNKS, OUT_CHUNKS = IN_WIDTH // CW, D_MODEL // CW
COL = dict(qa=0, ka=WIDTH_A, va=2 * WIDTH_A, qb=3 * WIDTH_A, kb=3 * WIDTH_A + WIDTH_B,
           vb=3 * WIDTH_A + WIDTH_B + KV_WIDTH)
H_WIDTH = COL["vb"] + KV_WIDTH
CHUNKS = IN_CHUNKS + OUT_CHUNKS
ORDER = [10, 8, 9, 11, 12, 0, 1, 2, 3, 4, 5, 6, 7]
KEYS_B = 10
NORM_CHUNKS = 3
FIRST_A = 5
NORM, ROPE, VALUE, GATE = range(4)
KIND = {8: NORM, 9: NORM, 10: NORM, 11: GATE, 12: GATE, 0: ROPE, 1: ROPE, 2: ROPE, 3: ROPE,
        4: VALUE, 5: VALUE, 6: GATE, 7: GATE}

HOME = {10: COL["kb"], 8: COL["qb"], 9: COL["qb"] + CW, 11: 4, 12: 6, 0: 0, 1: CW, 2: 2 * CW, 3: 3 * CW,
        4: 4 * CW, 5: 5 * CW, 6: 0, 7: 2}

SLICES = KT // 2
RAW = 2
RING = 7
HEADS = N_HEADS_B + N_HEADS_A
UNITS = QT + 1
NU = HEADS * UNITS
PRING = 3

MASK_W = (QT - 1) * P + SEQ
C_IDENT, C_MASK = 0, P
C_COSA = C_MASK + MASK_W
C_SINA = C_COSA + QT * HEAD_DIM
C_COSB = C_SINA + QT * HEAD_DIM
C_SINB = C_COSB + QT * HEAD_DIM
C_W = C_SINB + QT * HEAD_DIM


def shape_constants():
    c = np.zeros((P, C_W), np.float32)
    c[:, C_IDENT:C_IDENT + P] = np.eye(P, dtype=np.float32)
    dist = np.arange(P)[:, None] - np.arange(MASK_W)[None, :] + (QT - 1) * P
    count = sum(((dist % dil == 0) & (abs(dist) <= dil * (window // (2 * dil)))).astype(np.int64)
                for window, dil in DILATED_PATTERNS)
    c[:, C_MASK:C_MASK + MASK_W] = np.where(count > 0, np.log(np.maximum(count, 1)) / SCALE, NEG_BIG)

    def angles(pos, dim):
        inv = 1.0 / (np.float32(ROPE_THETA) ** (np.arange(0, dim, 2, dtype=np.float32) / np.float32(dim)))
        a = pos.astype(np.float32)[:, None] * inv.astype(np.float32)[None, :]
        a = np.concatenate([a, a], -1)
        sign = np.where(np.arange(dim) < dim // 2, -1.0, 1.0)
        return np.cos(a), np.sin(a) * sign

    pos = np.arange(SEQ)
    cos_a, sin_a = angles(pos, HEAD_DIM)
    rows, cols = angles(pos // GRID_W, HEAD_DIM // 2), angles(pos % GRID_W, HEAD_DIM // 2)
    cos_b, sin_b = (np.concatenate([r, k], -1) for r, k in zip(rows, cols))
    for at, table in ((C_COSA, cos_a), (C_SINA, sin_a), (C_COSB, cos_b), (C_SINB, sin_b)):
        c[:, at:at + QT * HEAD_DIM] = table.reshape(QT, P, HEAD_DIM).transpose(1, 0, 2).reshape(P, -1)
    return c


def head_columns(j):
    if j < N_HEADS_B:
        kv = j // (N_HEADS_B // N_KV_B)
        return (COL["qb"] + 64 * j, COL["kb"] + 64 * kv, COL["vb"] + 64 * kv,
                (WIDTH_A + 64 * j) // P, kv, False)
    h = j - N_HEADS_B
    return (COL["qa"] + 64 * h, COL["ka"] + 64 * h, COL["va"] + 64 * h, 64 * h // P, N_KV_B + h, True)


def build(nc, x_prompt, x_sample, w_in, w_out, q_norm, k_norm, ln_g, ln_b, consts, y_prompt, y_sample):
    ctx = ExitStack()
    with ctx:
        def sb(name, shape, dt=F32):
            return ctx.enter_context(nc.sbuf_tensor(name, shape, dt))

        def sem(name):
            return ctx.enter_context(nc.semaphore(name))

        t_hi = sb("t_hi", [P, KT, TOK], F32R)
        t_lo = sb("t_lo", [P, KT, TOK], F32R)
        w_hi = sb("w_hi", [P, RING, 2, CW], F32R)
        w_lo = sb("w_lo", [P, RING, 2, CW], F32R)
        q_st = sb("q_st", [P, 2, TOK], F32R)
        k_hi = sb("k_hi", [P, 2, TOK], F32R)
        k_lo = sb("k_lo", [P, 2, TOK], F32R)
        v_st = sb("v_st", [P, 2, TILES, 2 * HEAD_DIM], F32R)
        k_two = sb("k_two", [P, TILES, 2 * HEAD_DIM])
        p_hi = sb("p_hi", [P, 2, SEQ], F32R)
        p_lo = sb("p_lo", [P, 2, SEQ], F32R)
        h = sb("h", [P, TILES, H_WIDTH])
        mix_t = sb("mix_t", [P, KT, TOK])
        raw = sb("raw", [P, RAW, 2, CW])
        cst = sb("cst", [P, C_W])
        cosg = sb("cosg", [P, 2, QT, HEAD_DIM])
        sing = sb("sing", [P, 2, QT, HEAD_DIM])
        tmp_c = sb("tmp_c", [P, 2, CW])
        tmp_s = sb("tmp_s", [P, 2, CW])
        prob = sb("prob", [P, PRING, SEQ])
        tanh = sb("tanh", [P, 2, SEQ])
        nmax = sb("nmax", [P, HEADS, TILES])
        den = sb("den", [P, HEADS, TILES])
        rden = sb("rden", [P, HEADS, TILES])
        norms = sb("norms", [P, 2, HEAD_DIM])
        ssq = sb("ssq", [P, 2, TILES, HPC])
        squares = tanh[:, :, 0:CW]
        rstd = sb("rstd", [P, 2, TILES * HPC])
        stats = sb("stats", [P, TILES, OUT_CHUNKS, 6])
        mv = sb("mv", [P, TILES, 2])
        lnr = sb("lnr", [P, TILES, 4])
        half = sb("half", [P, TILES * HPC])
        zero = sb("zero", [P, 1])
        scr = sb("scr", [P, TILES * HPC])

        ident = cst[:, C_IDENT:C_IDENT + P]

        def table(at, t):
            k = t if t < QT else t - QT
            return cst[:, at + k * HEAD_DIM:at + (k + 1) * HEAD_DIM]

        bank = [ctx.enter_context(nc.psum_tensor(f"bank{i}", [P, 512], F32)) for i in range(8)]
        acc, s_ps, pt_ps, o_ps, t_ps = bank[0:2], bank[2:4], bank[4:6], bank[6], bank[7]

        x_loaded = [sem(f"x_loaded{t}") for t in range(TILES)]
        consts_loaded = sem("consts_loaded")
        norms_loaded = sem("norms_loaded")
        raw_loaded = [sem(f"raw_loaded{i}") for i in range(RAW)]
        hi_done = sem("w_hi_done")
        lo_done = sem("w_lo_done")
        tables_ready = sem("tables_ready")
        pool_consts = sem("pool_consts")
        xt_written, xt_hi, xt_lo = sem("xt_written"), sem("xt_hi"), sem("xt_lo")
        acc_ready = sem("acc_ready")
        act_evacuated, dve_evacuated = sem("act_evacuated"), sem("dve_evacuated")
        tanh_done = sem("tanh_done")
        products_ready, rope_added = sem("products_ready"), sem("rope_added")
        squared, summed, rstd_ready, normed = sem("squared"), sem("summed"), sem("rstd_ready"), sem("normed")
        pool_step, dve_step = sem("pool_step"), sem("dve_step")
        t_written, t_hi_done, t_lo_done = sem("t_written"), sem("t_hi_done"), sem("t_lo_done")
        v_split, keys_doubled = sem("v_split"), sem("keys_doubled")
        s_ready, s_masked = sem("s_ready"), sem("s_masked")
        exp_done = sem("exp_done")
        pt_ready, pt_hi_done, pt_lo_done = sem("pt_ready"), sem("pt_hi_done"), sem("pt_lo_done")
        pv_done = sem("pv_done")
        den_inverted, scaled, mixed = sem("den_inverted"), sem("scaled"), sem("mixed")
        mix_hi, mix_lo = sem("mix_hi"), sem("mix_lo")
        slice_used = sem("slice_used")
        xres_loaded = sem("xres_loaded")
        ln_loaded = sem("ln_loaded")
        stats_ready, ln_rstd, ln_normed, ln_scaled, y_ready = (
            sem("stats_ready"), sem("ln_rstd"), sem("ln_normed"), sem("ln_scaled"), sem("y_ready"))
        stored = sem("stored")

        block = ctx.enter_context(nc.Block())

        AHEAD = (IN_CHUNKS + 1) * SLICES + RAW

        def kind_of(c):
            return KIND[ORDER[c]] if c < IN_CHUNKS else None

        parts = [2 * (CW // P) if kind_of(c) == GATE else TILES for c in range(CHUNKS)]
        items = [(c, n) for c in range(CHUNKS) for n in range(parts[c])]
        index = {item: i for i, item in enumerate(items)}
        IN_ITEMS = index[(IN_CHUNKS, 0)]
        evac = []
        n_act = n_dve = n_rot = 0
        for c, n in items:
            n_rot += kind_of(c) in (NORM, ROPE)
            if kind_of(c) in (NORM, VALUE):
                n_act += 1
                evac.append((act_evacuated, n_act))
            elif kind_of(c) == ROPE:
                evac.append((products_ready, n_rot))
            else:
                n_dve += 1
                evac.append((dve_evacuated, n_dve))
        gates = [item for item in items if kind_of(item[0]) == GATE]
        ropes = [item for item in items if kind_of(item[0]) in (NORM, ROPE)]
        A_ITEMS = [item for item in items if FIRST_A <= item[0] < IN_CHUNKS]
        assert len(A_ITEMS) <= NU

        def late_tiles(c, n):
            return range(n * TILES // parts[c], (n + 1) * TILES // parts[c])

        def slices_at(c, n):
            at = {1: [0], 2: [1], 3: [2], 5: [3]} if parts[c] == TILES else {0: [0], 1: [1], 2: [2], 3: [3]}
            return [(c + 1) * SLICES + s for s in at.get(n, [])]

        def chunk_source(c):
            if c < IN_CHUNKS:
                w, at = w_in, ORDER[c] * CW
            else:
                w, at = w_out, (c - IN_CHUNKS) * CW
            return w[:, at:at + CW].rearrange("(k p) n -> p k n", p=P)

        def x_rows(t):
            return x_prompt[t * P:(t + 1) * P, :] if t < QT else x_sample[(t - QT) * P:(t - QT + 1) * P, :]

        def y_rows(t):
            return y_prompt[t * P:(t + 1) * P, :] if t < QT else y_sample[(t - QT) * P:(t - QT + 1) * P, :]

        own_kv = [j == 0 or head_columns(j)[4] != head_columns(j - 1)[4] for j in range(HEADS)]

        def staging(j):
            return [("q", j)] + ([("k", j)] if own_kv[j] else []) + [("r", j)]

        steps = {u: [] for u in range(NU + 3)}
        for j in range(HEADS - 1):
            for n, b in enumerate(staging(j + 1)):
                steps[UNITS * j + (0, 2, 3)[n]].append(b)
        first = staging(0)
        t_count = {}
        for b in first + [b for u in range(NU + 3) for b in steps[u]]:
            t_count[b] = len(t_count)
        staged = [t_count[staging(j)[-1]] + 1 for j in range(HEADS)]

        split_at = {len(A_ITEMS) + 1 + 2 * n: N_HEADS_A // 2 + n for n in range(N_HEADS_B // 2)}
        split_at.update({UNITS * j + 8: (j - N_HEADS_B) // 2 for j in range(N_HEADS_B + 1, HEADS, 2)})
        split_order = [split_at[u] for u in sorted(split_at)]

        def mixes_at(u):
            j, k = divmod(u - UNITS, UNITS)
            return [(j, k - 1)] if k in (1, 2) and 0 <= j < HEADS else []

        def mixed_through(j):
            return 2 * (j + 1)

        def norm_heads(c):
            return N_KV_B if ORDER[c] == KEYS_B else HPC

        @block.sync
        def _(sp):
            def load_slice(g):
                if g >= RAW:
                    sp.wait_ge(lo_done, g - RAW + 1)
                c, s = divmod(g, SLICES)
                sp.dma_start(raw[:, g % RAW, :, :], chunk_source(c)[:, 2 * s:2 * s + 2, :]) \
                    .then_inc(raw_loaded[g % RAW], 16)

            for t in range(TILES):
                sp.dma_start(h[:, t, 0:D_MODEL], x_rows(t)).then_inc(x_loaded[t], 16)
                if t < RAW:
                    load_slice(t)
            for g in range(RAW, AHEAD):
                load_slice(g)
            sp.wait_ge(t_written, staged[HEADS - 1])
            sp.wait_ge(v_split, HEADS // 2 + N_KV_B)
            for t in range(TILES):
                sp.dma_start(h[:, t, 0:D_MODEL], x_rows(t)).then_inc(xres_loaded, 16)
            for n, src in enumerate((ln_g, ln_b)):
                for k in range(2):
                    sp.dma_start(h[:, 2 * n + k, 2 * WIDTH_A:3 * WIDTH_A],
                                 src[None, k * 512:(k + 1) * 512].to_broadcast([P, 512])).then_inc(ln_loaded, 16)
            for g in range(AHEAD, CHUNKS * SLICES):
                load_slice(g)
            for t in range(TILES):
                sp.wait_ge(y_ready, t + 1)
                sp.dma_start(y_rows(t), h[:, t, 0:D_MODEL]).then_inc(stored, 16)
            sp.wait_ge(stored, 16 * TILES)

        @block.tensor
        def _(pe):
            def transpose_batch(dst, pieces):
                for n, src in enumerate(pieces):
                    ins = nc.tensor.transpose(dst[0:src.shape[-1], n * P:(n + 1) * P], src, ident)
                return ins

            def x_transposes(t):
                pe.wait_ge(x_loaded[t], 16)
                for b in range(2):
                    i = 2 * t + b
                    if i >= 2:
                        pe.wait_ge(xt_lo, i - 1)
                    transpose_batch(pt_ps[i % 2], [h[:, t, (4 * b + n) * P:(4 * b + n + 1) * P] for n in range(4)]) \
                        .then_inc(xt_written, 1)

            def project(c, n):
                i = index[(c, n)]
                if i >= 2:
                    pe.wait_ge(*evac[i - 2])
                for k in range(KT):
                    g = c * SLICES + k // 2
                    if n == 0 and k % 2 == 0:
                        pe.wait_ge(lo_done, g + 1)
                    w_h, w_l = w_hi[:, g % RING, k % 2, :], w_lo[:, g % RING, k % 2, :]
                    if kind_of(c) == GATE:
                        e, cols = n // 2, slice(0, SEQ) if n % 2 == 0 else slice(SEQ, TOK)
                        a_hi, a_lo = w_h[:, e * P:(e + 1) * P], w_l[:, e * P:(e + 1) * P]
                        b_hi, b_lo = t_hi[:, k, cols], t_lo[:, k, cols]
                        out = acc[i % 2][:, 0:cols.stop - cols.start]
                    else:
                        a_hi, a_lo = t_hi[:, k, n * P:(n + 1) * P], t_lo[:, k, n * P:(n + 1) * P]
                        b_hi, b_lo = w_h, w_l
                        out = acc[i % 2][:, 0:CW]
                    nc.tensor.matmul(out, a_lo, b_hi, start=(k == 0), stop=False)
                    nc.tensor.matmul(out, a_hi, b_lo, start=False, stop=False)
                    ins = nc.tensor.matmul(out, a_hi, b_hi, start=False, stop=(k == KT - 1))
                    if n == parts[c] - 1 and k % 2 == 1 and k < KT - 1:
                        ins.then_inc(slice_used, 1)
                ins.then_inc(acc_ready, 1)

            def t_batch(b):
                n = t_count[b]
                if n:
                    pe.wait_ge(t_lo_done, n)
                qc, kc, _, _, kv, _ = head_columns(b[1])
                if b[0] == "q":
                    pieces = [h[:, t, qc:qc + HEAD_DIM] for t in range(QT)]
                elif b[0] == "k":
                    pe.wait_ge(keys_doubled, kv + 1)
                    pieces = [k_two[:, t, :] for t in range(QT)]
                else:
                    pieces = [h[:, QT + t, qc:qc + HEAD_DIM] for t in range(ST)]
                    if own_kv[b[1]]:
                        pieces += [k_two[:, QT + t, :] for t in range(ST)]
                transpose_batch(t_ps, pieces).then_inc(t_written, 1)

            def scores(u):
                j, k = divmod(u, UNITS)
                kv = head_columns(j)[4]
                if k == 0:
                    pe.wait_ge(t_lo_done, staged[j])
                if u >= 2:
                    pe.wait_ge(s_masked, u - 1)
                out = s_ps[u % 2]
                q = q_st[:, j % 2, :]
                if k < QT:
                    nc.tensor.matmul(out[:], q[:, k * P:(k + 1) * P], k_lo[:, kv % 2, 0:SEQ], start=True, stop=False)
                    ins = nc.tensor.matmul(out[:], q[:, k * P:(k + 1) * P], k_hi[:, kv % 2, 0:SEQ],
                                           start=False, stop=True)
                else:
                    for t in range(ST):
                        o = out[:, t * DEC_SEQ:(t + 1) * DEC_SEQ]
                        lhs = q[:, SEQ + t * P:SEQ + (t + 1) * P]
                        nc.tensor.matmul(o, lhs, k_lo[:, kv % 2, SEQ:TOK], start=True, stop=False)
                        ins = nc.tensor.matmul(o, lhs, k_hi[:, kv % 2, SEQ:TOK], start=False, stop=True)
                ins.then_inc(s_ready, 1)

            def prob_transposes(u):
                pe.wait_ge(scaled, u + 1)
                if u >= 2:
                    pe.wait_ge(pt_lo_done, u - 1)
                transpose_batch(pt_ps[u % 2], [prob[:, u % PRING, n * P:(n + 1) * P] for n in range(4)]) \
                    .then_inc(pt_ready, 1)

            def values(u):
                j, k = divmod(u, UNITS)
                kv = head_columns(j)[4]
                if k == 0:
                    pe.wait_ge(v_split, kv + 1)
                    if j:
                        pe.wait_ge(mixed, mixed_through(j - 1))
                if k == QT:
                    pe.wait_ge(mixed, mixed_through(j) - 1)
                pe.wait_ge(pt_lo_done, u + 1)
                groups = [(k, 0, QT, 0)] if k < QT else [(t, QT, ST, t * ST) for t in range(ST)]
                for t, base, keys, piece in groups:
                    o = o_ps[0:HEAD_DIM, t * P:(t + 1) * P]
                    for n in range(keys):
                        cols = slice((piece + n) * P, (piece + n + 1) * P)
                        vh = v_st[:, kv % 2, base + n, 0:HEAD_DIM]
                        vl = v_st[:, kv % 2, base + n, HEAD_DIM:2 * HEAD_DIM]
                        nc.tensor.matmul(o, vh, p_lo[:, u % 2, cols], start=(n == 0), stop=False)
                        nc.tensor.matmul(o, vl, p_hi[:, u % 2, cols], start=False, stop=False)
                        ins = nc.tensor.matmul(o, vh, p_hi[:, u % 2, cols], start=False, stop=(n == keys - 1))
                ins.then_inc(pv_done, 1)

            pe.wait_ge(consts_loaded, 16)
            x_transposes(0)
            for t in range(TILES):
                if t + 1 < TILES:
                    x_transposes(t + 1)
                pe.wait_ge(xt_lo, 2 * t + 2)
                project(0, t)
            for c in range(1, FIRST_A):
                for n in range(parts[c]):
                    project(c, n)
            pe.wait_ge(rope_added, NORM_CHUNKS * TILES)
            for b in first:
                t_batch(b)
            for u in range(NU + 3):
                if u == UNITS * (N_HEADS_B - 1):
                    pe.wait_ge(rope_added, len(ropes))
                if u < NU:
                    scores(u)
                for b in steps[u]:
                    t_batch(b)
                if 2 <= u < NU + 2:
                    prob_transposes(u - 2)
                if u >= 3:
                    values(u - 3)
                if u < len(A_ITEMS):
                    project(*A_ITEMS[u])
            pe.wait_ge(mix_lo, KT)
            for c in range(IN_CHUNKS, CHUNKS):
                for n in range(parts[c]):
                    project(c, n)

        def t_destination(b):
            j = b[1]
            kv = head_columns(j)[4]
            if b[0] == "q":
                return [(0, SEQ, q_st[0:HEAD_DIM, j % 2, 0:SEQ])]
            if b[0] == "k":
                return [(0, SEQ, k_hi[:, kv % 2, 0:SEQ])]
            out = [(0, DEC_SEQ, q_st[0:HEAD_DIM, j % 2, SEQ:TOK])]
            if own_kv[j]:
                out.append((DEC_SEQ, 2 * DEC_SEQ, k_hi[:, kv % 2, SEQ:TOK]))
            return out

        @block.scalar
        def _(act):
            act.dma_start(cst[:], consts[:, :]).then_inc(consts_loaded, 16)
            act.dma_start(norms[:, 0, :], q_norm[None, :].to_broadcast([P, HEAD_DIM])).then_inc(norms_loaded, 16)
            act.dma_start(norms[:, 1, :], k_norm[None, :].to_broadcast([P, HEAD_DIM])).then_inc(norms_loaded, 16)

            def weights_high(g):
                act.wait_ge(raw_loaded[g % RAW], 16 * (g // RAW + 1))
                if g >= RING:
                    c, s = divmod(g - RING, SLICES)
                    if s < SLICES - 1:
                        act.wait_ge(slice_used, (SLICES - 1) * c + s + 1)
                    else:
                        act.wait_ge(acc_ready, index[(c, parts[c] - 1)] + 1)
                nc.scalar.activation(w_hi[:, g % RING, :, :], raw[:, g % RAW, :, :], ACT.Copy).then_inc(hi_done, 1)

            def x_high(t):
                for b in range(2):
                    i = 2 * t + b
                    act.wait_ge(xt_written, i + 1)
                    nc.scalar.activation(t_hi[:, 4 * b:4 * b + 4, t * P:(t + 1) * P],
                                         pt_ps[i % 2][:].rearrange("p (n q) -> p n q", n=4), ACT.Copy) \
                        .then_inc(xt_hi, 1)

            def evacuate(c, n):
                i = index[(c, n)]
                kind = kind_of(c)
                if kind == ROPE:
                    return
                act.wait_ge(acc_ready, i + 1)
                if kind == GATE:
                    m = gates.index((c, n))
                    w = SEQ if n % 2 == 0 else DEC_SEQ
                    if m >= 2:
                        act.wait_ge(dve_evacuated, m - 1)
                    else:
                        act.wait_ge(summed, NORM_CHUNKS * TILES)
                    nc.scalar.activation(tanh[:, m % 2, 0:w], acc[i % 2][:, 0:w], ACT.Tanh, scale=0.5) \
                        .then_inc(tanh_done, 1)
                else:
                    at = HOME[ORDER[c]]
                    nc.scalar.activation(h[:, n, at:at + CW], acc[i % 2][:, 0:CW], ACT.Copy).then_inc(act_evacuated, 1)

            def t_high(b):
                n = t_count[b]
                act.wait_ge(t_written, n + 1)
                if b[0] in ("q", "k"):
                    j = b[1]
                    if j >= 2:
                        act.wait_ge(s_ready, UNITS * (j - 1))
                for a, z, dst in t_destination(b):
                    ins = nc.scalar.activation(dst, t_ps[0:dst.shape[0], a:z], ACT.Copy)
                ins.then_inc(t_hi_done, 1)

            def exps(u):
                j, k = divmod(u, UNITS)
                act.wait_ge(s_masked, u + 1)
                rows = [(k, 0, SEQ)] if k < QT else [(QT + t, t * DEC_SEQ, (t + 1) * DEC_SEQ) for t in range(ST)]
                for t, a, z in rows:
                    s = prob[:, u % PRING, a:z]
                    ins = nc.scalar.activation(s, s, ACT.Exp, scale=-1.0, bias=nmax[:, j, t:t + 1],
                                               accum_out=den[:, j, t:t + 1])
                ins.then_inc(exp_done, 1)

            def prob_high(u):
                act.wait_ge(pt_ready, u + 1)
                if u >= 2:
                    act.wait_ge(pv_done, u - 1)
                nc.scalar.activation(p_hi[:, u % 2, :], pt_ps[u % 2][:], ACT.Copy).then_inc(pt_hi_done, 1)

            def split_mixed(n):
                e = split_order[n]
                if n == 0:
                    act.wait_ge(acc_ready, IN_ITEMS)
                j = 2 * e - N_HEADS_A if e >= N_HEADS_A // 2 else 2 * e + N_HEADS_B
                act.wait_ge(mixed, mixed_through(j + 1))
                nc.scalar.activation(t_hi[:, e, :], mix_t[:, e, :], ACT.Copy).then_inc(mix_hi, 1)

            for g in range(2):
                weights_high(g)
            x_high(0)
            for g in range(2, 4):
                weights_high(g)
            for t in range(1, TILES):
                x_high(t)
                for g in slices_at(0, t):
                    weights_high(g)
                evacuate(0, t - 1)
            evacuate(0, TILES - 1)
            for c in range(1, FIRST_A):
                for n in range(parts[c]):
                    for g in slices_at(c, n):
                        weights_high(g)
                    evacuate(c, n)
            for b in first:
                t_high(b)
            for u in range(NU + 3):
                for b in steps[u]:
                    t_high(b)
                if 2 <= u < NU + 2:
                    prob_high(u - 2)
                if u < NU:
                    exps(u)
                if u < len(A_ITEMS):
                    c, n = A_ITEMS[u]
                    for g in slices_at(c, n):
                        weights_high(g)
                    evacuate(c, n)
                if u in split_at:
                    split_mixed(split_order.index(split_at[u]))
            split_mixed(KT - 1) if max(split_at) >= NU + 3 else None
            for g in range((IN_CHUNKS + 1) * SLICES, CHUNKS * SLICES):
                weights_high(g)
            for t in range(TILES):
                act.wait_ge(ln_rstd, t + 1)
                r = h[:, t, 0:D_MODEL]
                nc.scalar.activation(r, r, ACT.Identity, scale=lnr[:, t, 0:1], bias=lnr[:, t, 1:2]) \
                    .then_inc(ln_normed, 1)

        @block.vector
        def _(dve):
            links = [0]

            def after(ins):
                links[0] += 1
                ins.then_inc(dve_step, 1)
                dve.wait_ge(dve_step, links[0])

            def swap_halves(out, in_, tab, heads, block_w):
                n = HEAD_DIM // block_w
                w = block_w // 2
                for a, b in ((0, w), (w, 0)):
                    for k in range(n):
                        o = out.rearrange("p (m d) -> p m d", d=HEAD_DIM)[:, :, k * block_w + a:k * block_w + a + w]
                        i = in_.rearrange("p (m d) -> p m d", d=HEAD_DIM)[:, :, k * block_w + b:k * block_w + b + w]
                        tt = tab[:, None, k * block_w + a:k * block_w + a + w].to_broadcast([P, heads, w])
                        ins = nc.vector.tensor_tensor(o, i, tt, ALU.mult)
                return ins

            def heads_of(ap):
                return ap.rearrange("p (m d) -> p m d", d=HEAD_DIM)

            def x_low(t):
                for b in range(2):
                    i = 2 * t + b
                    dve.wait_ge(xt_hi, i + 1)
                    at = t_hi[:, 4 * b:4 * b + 4, t * P:(t + 1) * P]
                    nc.vector.tensor_tensor(t_lo[:, 4 * b:4 * b + 4, t * P:(t + 1) * P],
                                            pt_ps[i % 2][:].rearrange("p (n q) -> p n q", n=4),
                                            at.bitcast(F32), ALU.subtract).then_inc(xt_lo, 1)

            def rotate(src, cos, sin, heads, block_w, n):
                if n >= 2:
                    dve.wait_ge(rope_added, n - 1)
                nc.vector.tensor_tensor(heads_of(tmp_c[:, n % 2, 0:heads * HEAD_DIM]), heads_of(src),
                                        cos[:, None, :].to_broadcast([P, heads, HEAD_DIM]), ALU.mult)
                ins = swap_halves(tmp_s[:, n % 2, 0:heads * HEAD_DIM], src, sin, heads, block_w)
                ins.then_inc(products_ready, 1)

            def sums(c, t):
                n = c * TILES + t
                dve.wait_ge(squared, n + 1)
                m = norm_heads(c)
                nc.vector.reduce_sum(ssq[:, c % 2, t, 0:m], heads_of(squares[:, n % 2, 0:m * HEAD_DIM]), axis=AX.X) \
                    .then_inc(summed, 1)

            def norm_and_rotate(c, t):
                which = 1 if ORDER[c] == KEYS_B else 0
                m = norm_heads(c)
                dve.wait_ge(rstd_ready, c + 1)
                at = HOME[ORDER[c]]
                src = h[:, t, at:at + m * HEAD_DIM]
                k = t if t < QT else t - QT
                r = rstd[:, c % 2, t * HPC:t * HPC + m]
                after(nc.vector.tensor_tensor(heads_of(src), heads_of(src),
                                              r[:, :, None].to_broadcast([P, m, HEAD_DIM]), ALU.mult))
                rotate(src, cosg[:, which, k, :], sing[:, which, k, :], m, HEAD_DIM // 2, c * TILES + t)

            def evacuate(c, n):
                i = index[(c, n)]
                if kind_of(c) == GATE:
                    m = gates.index((c, n))
                    cols = slice(0, SEQ) if n % 2 == 0 else slice(SEQ, TOK)
                    w = cols.stop - cols.start
                    dve.wait_ge(tanh_done, m + 1)
                    nc.vector.scalar_tensor_tensor(
                        out=mix_t[:, HOME[ORDER[c]] + n // 2, cols], in0=tanh[:, m % 2, 0:w], scalar=1.0,
                        in1=acc[i % 2][:, 0:w], op0=ALU.add, op1=ALU.mult).then_inc(dve_evacuated, 1)
                elif kind_of(c) == ROPE:
                    dve.wait_ge(acc_ready, i + 1)
                    rotate(acc[i % 2][:, 0:CW], table(C_COSA, n), table(C_SINA, n), HPC, HEAD_DIM,
                           ropes.index((c, n)))

            def mask_max(u):
                j, k = divmod(u, UNITS)
                is_a = head_columns(j)[5]
                dve.wait_ge(s_ready, u + 1)
                if u >= PRING:
                    dve.wait_ge(pt_ready, u - PRING + 1)
                rows = [(k, 0, SEQ)] if k < QT else [(QT + t, t * DEC_SEQ, (t + 1) * DEC_SEQ) for t in range(ST)]
                for t, a, z in rows:
                    if is_a:
                        m0 = C_MASK + (QT - 1 - (t if t < QT else t - QT)) * P
                        mask = cst[:, m0:m0 + z - a]
                    else:
                        mask = zero[:].to_broadcast([P, z - a])
                    ins = nc.vector.tensor_tensor_reduce(
                        out=prob[:, u % PRING, a:z], in0=s_ps[u % 2][:, a:z], in1=mask, scale=-SCALE,
                        scalar=-NEG_BIG, op0=ALU.add, op1=ALU.min, accum_out=nmax[:, j, t:t + 1])
                ins.then_inc(s_masked, 1)

            def prob_low(u):
                dve.wait_ge(pt_hi_done, u + 1)
                nc.vector.tensor_tensor(p_lo[:, u % 2, :], pt_ps[u % 2][:], p_hi[:, u % 2, :].bitcast(F32),
                                        ALU.subtract).then_inc(pt_lo_done, 1)

            def t_low(b):
                n = t_count[b]
                dve.wait_ge(t_hi_done, n + 1)
                for a, z, dst in t_destination(b):
                    if b[0] == "k" or a:
                        kv = head_columns(b[1])[4]
                        lo = k_lo[:, kv % 2, 0:SEQ] if b[0] == "k" else k_lo[:, kv % 2, SEQ:TOK]
                        ins = nc.vector.tensor_tensor(lo, t_ps[:, a:z], dst.bitcast(F32), ALU.subtract)
                    else:
                        low = q_st[HEAD_DIM:P, b[1] % 2, 0:SEQ] if b[0] == "q" else \
                            q_st[HEAD_DIM:P, b[1] % 2, SEQ:TOK]
                        ins = nc.vector.tensor_tensor(low, t_ps[0:HEAD_DIM, a:z], dst.bitcast(F32), ALU.subtract)
                ins.then_inc(t_lo_done, 1)

            def invert(u):
                j, k = divmod(u, UNITS)
                t = slice(k, k + 1) if k < QT else slice(QT, TILES)
                dve.wait_ge(exp_done, u + 1)
                nc.vector.reciprocal(rden[:, j, t], den[:, j, t]).then_inc(den_inverted, 1)

            def mix(j, part):
                e = head_columns(j)[3]
                rows = slice(HEAD_DIM * (j % 2), HEAD_DIM * (j % 2) + HEAD_DIM)
                cols = slice(0, SEQ) if part == 0 else slice(SEQ, TOK)
                dve.wait_ge(pv_done, UNITS * j + QT + part)
                g = mix_t[rows, e, cols]
                nc.vector.tensor_tensor(g, o_ps[0:HEAD_DIM, 0:cols.stop - cols.start], g, ALU.mult).then_inc(mixed, 1)

            nc.vector.memset(zero[:], 0.0)
            nc.vector.memset(half[:], -0.5).then_inc(pool_consts, 1)
            dve.wait_ge(consts_loaded, 16)
            dve.wait_ge(norms_loaded, 32)
            for w in range(2):
                g = norms[:, w, :]
                nc.vector.tensor_tensor(cosg[:, w], cst[:, C_COSB:C_COSB + QT * HEAD_DIM]
                                        .rearrange("p (t d) -> p t d", d=HEAD_DIM),
                                        g[:, None, :].to_broadcast([P, QT, HEAD_DIM]), ALU.mult)
                sin = cst[:, C_SINB:C_SINB + QT * HEAD_DIM].rearrange("p (t d) -> p t d", d=HEAD_DIM)
                q = HEAD_DIM // 4
                for k in range(4):
                    o = k ^ 1
                    nc.vector.tensor_tensor(sing[:, w, :, k * q:(k + 1) * q], sin[:, :, k * q:(k + 1) * q],
                                            g[:, None, o * q:(o + 1) * q].to_broadcast([P, QT, q]), ALU.mult) \
                        .then_inc(tables_ready, 1)
            dve.wait_ge(tables_ready, 8)
            x_low(0)
            for t in range(1, TILES):
                x_low(t)
                sums(0, t - 1)
            sums(0, TILES - 1)
            for c in range(1, FIRST_A):
                for n in range(parts[c]):
                    if c < NORM_CHUNKS:
                        sums(c, n)
                    if c <= NORM_CHUNKS:
                        for t in late_tiles(c, n):
                            norm_and_rotate(c - 1, t)
                    evacuate(c, n)
            for b in first:
                t_low(b)
            for u in range(NU + 3):
                if 1 <= u < NU + 1:
                    invert(u - 1)
                if u < NU:
                    mask_max(u)
                for b in steps[u]:
                    t_low(b)
                if 2 <= u < NU + 2:
                    prob_low(u - 2)
                for m in mixes_at(u):
                    mix(*m)
                if u < len(A_ITEMS):
                    evacuate(*A_ITEMS[u])
            for c in range(OUT_CHUNKS):
                for t in range(TILES):
                    i = index[(IN_CHUNKS + c, t)]
                    r = h[:, t, c * CW:(c + 1) * CW]
                    dve.wait_ge(acc_ready, i + 1)
                    if c == 0 and t == 0:
                        dve.wait_ge(xres_loaded, 16 * TILES)
                    after(nc.vector.scalar_tensor_tensor(out=r, in0=r, scalar=ALPHA, in1=acc[i % 2][:, 0:CW],
                                                         op0=ALU.mult, op1=ALU.add))
                    last_i = nc.vector.bn_stats(stats[:, t, c, :], r)
                    last_i.then_inc(dve_evacuated, 1)
                    if c == OUT_CHUNKS - 1:
                        dve.wait_ge(dve_evacuated, evac[i][1])
                        nc.vector.bn_aggr(mv[:, t, :], stats[:, t, :, :]).then_inc(stats_ready, 1)
            dve.wait_ge(ln_loaded, 64)
            for t in range(TILES):
                dve.wait_ge(ln_normed, t + 1)
                for k in range(2):
                    r = h[:, t, k * 512:(k + 1) * 512]
                    after(nc.vector.tensor_tensor(r, r, h[:, k, 2 * WIDTH_A:3 * WIDTH_A], ALU.mult))
                    ins = nc.vector.tensor_tensor(r, r, h[:, 2 + k, 2 * WIDTH_A:3 * WIDTH_A], ALU.add)
                ins.then_inc(y_ready, 1)

        @block.gpsimd
        def _(pool):
            links = [0]

            def after(ins):
                links[0] += 1
                ins.then_inc(pool_step, 1)
                pool.wait_ge(pool_step, links[0])

            def inverse_root(out, v, y, power):
                after(nc.gpsimd.tensor_tensor(y, v, power, ALU.pow))
                after(nc.gpsimd.tensor_tensor(out, y, y, ALU.mult))
                after(nc.gpsimd.tensor_tensor(out, out, v, ALU.mult))
                after(nc.gpsimd.tensor_scalar(out, out, -0.5, 1.5, ALU.mult, ALU.add))
                return nc.gpsimd.tensor_tensor(out, out, y, ALU.mult)

            def weights_low(g):
                pool.wait_ge(hi_done, g + 1)
                nc.gpsimd.tensor_tensor(w_lo[:, g % RING, :, :], raw[:, g % RAW, :, :],
                                        w_hi[:, g % RING, :, :].bitcast(F32), ALU.subtract).then_inc(lo_done, 1)

            def square(c, t):
                n = c * TILES + t
                m = norm_heads(c)
                pool.wait_ge(act_evacuated, n + 1)
                if n >= 2:
                    pool.wait_ge(summed, n - 1)
                at = HOME[ORDER[c]]
                src = h[:, t, at:at + m * HEAD_DIM]
                nc.gpsimd.tensor_tensor(squares[:, n % 2, 0:m * HEAD_DIM], src, src, ALU.mult).then_inc(squared, 1)

            def head_rstd(c):
                m = norm_heads(c)
                pool.wait_ge(summed, (c + 1) * TILES)
                if c >= 2:
                    pool.wait_ge(products_ready, (c - 1) * TILES)
                v = ssq[:, c % 2, :, 0:m]
                out, y, power = (a.rearrange("p (t m) -> p t m", m=HPC)[:, :, 0:m]
                                 for a in (rstd[:, c % 2, :], scr[:], half[:]))
                after(nc.gpsimd.tensor_scalar(v, v, 1.0 / HEAD_DIM, RMS_EPS, ALU.mult, ALU.add))
                inverse_root(out, v, y, power).then_inc(rstd_ready, 1)

            def add_rotation(c, t):
                n = ropes.index((c, t))
                m = norm_heads(c) if c < NORM_CHUNKS else HPC
                pool.wait_ge(products_ready, n + 1)
                if c == FIRST_A:
                    pool.wait_ge(xt_written, 2 * TILES)
                at = HOME[ORDER[c]]
                nc.gpsimd.tensor_tensor(h[:, t, at:at + m * HEAD_DIM], tmp_c[:, n % 2, 0:m * HEAD_DIM],
                                        tmp_s[:, n % 2, 0:m * HEAD_DIM], ALU.add).then_inc(rope_added, 1)

            def split_values(j):
                _, _, vc, _, kv, is_a = head_columns(j)
                pool.wait_ge(act_evacuated, n_act if is_a else NORM_CHUNKS * TILES)
                if kv >= 2:
                    pool.wait_ge(pv_done, UNITS * (N_HEADS_B // N_KV_B * (kv - 1) if kv <= N_KV_B else
                                                   N_HEADS_B + kv - 1 - N_KV_B))
                hi = v_st[:, kv % 2, :, 0:HEAD_DIM]
                src = h[:, :, vc:vc + HEAD_DIM]
                after(nc.gpsimd.tensor_scalar(hi, src, 1.0, 0.0, ALU.mult, ALU.add))
                nc.gpsimd.tensor_tensor(v_st[:, kv % 2, :, HEAD_DIM:2 * HEAD_DIM], src, hi.bitcast(F32),
                                        ALU.subtract).then_inc(v_split, 1)

            def double_keys(j):
                kc, kv, is_a = head_columns(j)[1], *head_columns(j)[4:6]
                pool.wait_ge(rope_added, len(ropes) if is_a else NORM_CHUNKS * TILES)
                if kv:
                    before = max(i for i in range(j) if own_kv[i])
                    pool.wait_ge(t_written, t_count[("r", before)] + 1)
                out = k_two[:].rearrange("p t (n d) -> p t n d", n=2)
                nc.gpsimd.tensor_scalar(out, h[:, :, None, kc:kc + HEAD_DIM].to_broadcast([P, TILES, 2, HEAD_DIM]),
                                        1.0, 0.0, ALU.mult, ALU.add).then_inc(keys_doubled, 1)

            def scale(u):
                j, k = divmod(u, UNITS)
                pool.wait_ge(den_inverted, u + 1)
                rows = [(k, 0, SEQ)] if k < QT else [(QT + t, t * DEC_SEQ, (t + 1) * DEC_SEQ) for t in range(ST)]
                for t, a, z in rows:
                    s = prob[:, u % PRING, a:z]
                    ins = nc.gpsimd.tensor_scalar(s, s, rden[:, j, t:t + 1], 0.5, ALU.mult, ALU.mult)
                ins.then_inc(scaled, 1)

            def mixed_low(n):
                e = split_order[n]
                pool.wait_ge(mix_hi, n + 1)
                nc.gpsimd.tensor_tensor(t_lo[:, e, :], mix_t[:, e, :], t_hi[:, e, :].bitcast(F32), ALU.subtract) \
                    .then_inc(mix_lo, 1)

            pool.wait_ge(pool_consts, 1)
            for g in range(4):
                weights_low(g)
            for t in range(TILES):
                for g in slices_at(0, t):
                    weights_low(g)
                square(0, t)
            head_rstd(0)
            for c in range(1, FIRST_A):
                for n in range(parts[c]):
                    for g in slices_at(c, n):
                        weights_low(g)
                    if c < NORM_CHUNKS:
                        square(c, n)
                    if c <= NORM_CHUNKS:
                        for t in late_tiles(c, n):
                            add_rotation(c - 1, t)
                if c < NORM_CHUNKS:
                    head_rstd(c)
            double_keys(0)
            split_values(0)
            for u in range(NU + 3):
                j, k = divmod(u, UNITS)
                if 1 <= u < NU + 1:
                    scale(u - 1)
                if j + 1 < HEADS and own_kv[j + 1] and k == 0:
                    double_keys(j + 1)
                if j + 1 < HEADS and own_kv[j + 1] and k == 4:
                    split_values(j + 1)
                if u < len(A_ITEMS):
                    c, n = A_ITEMS[u]
                    for g in slices_at(c, n):
                        weights_low(g)
                    if kind_of(c) == ROPE:
                        add_rotation(c, n)
                if u in split_at:
                    mixed_low(split_order.index(split_at[u]))
            mixed_low(KT - 1) if max(split_at) >= NU + 3 else None
            for g in range((IN_CHUNKS + 1) * SLICES, CHUNKS * SLICES):
                weights_low(g)
            for t in range(TILES):
                pool.wait_ge(stats_ready, t + 1)
                v, m = mv[:, t, 1:2], mv[:, t, 0:1]
                after(nc.gpsimd.tensor_scalar(lnr[:, t, 2:3], v, 1.0, LN_EPS, ALU.mult, ALU.add))
                after(inverse_root(lnr[:, t, 0:1], lnr[:, t, 2:3], lnr[:, t, 3:4], half[:, 0:1]))
                after(nc.gpsimd.tensor_tensor(lnr[:, t, 1:2], lnr[:, t, 0:1], m, ALU.mult))
                nc.gpsimd.tensor_scalar(lnr[:, t, 1:2], lnr[:, t, 1:2], -1.0, 0.0, ALU.mult, ALU.add) \
                    .then_inc(ln_rstd, 1)


def kernel(**inputs):
    import concourse.bacc as bacc
    from concourse.bass_utils import run_bass_kernel_spmd

    nc = bacc.Bacc("TRN2", target_bir_lowering=False, num_devices=1, dynamic_dma_scratch_size=1024)
    arrays = {
        "x_prompt": np.ascontiguousarray(inputs["x_prompt"][0]),
        "x_sample": np.ascontiguousarray(inputs["x_sample"][0]),
        "w_in": np.ascontiguousarray(inputs["w_in"][0]),
        "w_out": np.ascontiguousarray(inputs["w_out"][0]),
        "q_norm": np.ascontiguousarray(inputs["q_norm"][0]),
        "k_norm": np.ascontiguousarray(inputs["k_norm"][0]),
        "ln_g": np.ascontiguousarray(inputs["ln_g"][0]),
        "ln_b": np.ascontiguousarray(inputs["ln_b"][0]),
        "consts": shape_constants(),
    }
    args = [nc.dram_tensor(n, a.shape, F32, kind="ExternalInput").ap() for n, a in arrays.items()]
    args += [nc.dram_tensor(n, (s, D_MODEL), F32, kind="ExternalOutput").ap()
             for n, s in (("y_prompt", SEQ), ("y_sample", DEC_SEQ))]
    build(nc, *args)
    r = run_bass_kernel_spmd(nc, [arrays], core_ids=[0])
    return (r.results[0]["y_prompt"].reshape(1, SEQ, D_MODEL), r.results[0]["y_sample"].reshape(1, DEC_SEQ, D_MODEL))
```

```python
from contextlib import ExitStack

import numpy as np

import concourse.bass as bass
from concourse import mybir

F32 = mybir.dt.float32
F32R = mybir.dt.float32r
ALU = mybir.AluOpType
ACT = mybir.ActivationFunctionType
AX = mybir.AxisListType

P = 128
D_MODEL = 1024
SEQ, DEC_SEQ = 512, 256
HEAD_DIM = 64
N_HEADS_A, N_HEADS_B, N_KV_B = 8, 8, 2
WIDTH_A, WIDTH_B, KV_WIDTH = N_HEADS_A * HEAD_DIM, N_HEADS_B * HEAD_DIM, N_KV_B * HEAD_DIM
DILATED_PATTERNS = ((128, 1), (512, 4), (2048, 16))
GRID_W = 64
ROPE_THETA = 10000.0
LN_EPS, RMS_EPS = 1e-5, 1e-6
ALPHA = 2.0 ** 0.25
SCALE = HEAD_DIM ** -0.5
NEG_BIG = -1e30

QT = SEQ // P
ST = DEC_SEQ // P
TILES = QT + ST
TOK = TILES * P
KT = D_MODEL // P
CW = 256
HPC = CW // HEAD_DIM
IN_WIDTH = 4 * WIDTH_A + 2 * WIDTH_B + 2 * KV_WIDTH
IN_CHUNKS, OUT_CHUNKS = IN_WIDTH // CW, D_MODEL // CW
COL = dict(qa=0, ka=WIDTH_A, va=2 * WIDTH_A, qb=3 * WIDTH_A, kb=3 * WIDTH_A + WIDTH_B,
           vb=3 * WIDTH_A + WIDTH_B + KV_WIDTH)
H_WIDTH = COL["vb"] + KV_WIDTH
CHUNKS = IN_CHUNKS + OUT_CHUNKS
ORDER = [10, 8, 11, 9, 12, 0, 2, 4, 6, 1, 3, 5, 7]
KEYS_B = 10
ALONE = 3
NORM, ROPE, VALUE, GATE = range(4)
KIND = {8: NORM, 9: NORM, 10: NORM, 11: GATE, 12: GATE, 0: ROPE, 1: ROPE, 2: ROPE, 3: ROPE,
        4: VALUE, 5: VALUE, 6: GATE, 7: GATE}

HOME = {10: COL["kb"], 8: COL["qb"], 9: COL["qb"] + CW, 11: 4, 12: 6, 0: 0, 1: CW, 2: 2 * CW, 3: 3 * CW,
        4: 4 * CW, 5: 5 * CW, 6: 0, 7: 2}

SLICES = KT // 2
RAW = 2
RING = 6
HEADS = N_HEADS_B + N_HEADS_A
UNITS = QT + 1
NU = HEADS * UNITS
GROUPS = QT // 2 + 1
PRING = 4
CONSTS_AFTER = 2
DVE_LOW_CHUNKS = (0, 1, 2, 3)
LAG = 3
STEPS = NU + LAG + 1
BESIDE = ((0, 5), (3, 8), (55, 44), (62, 50), (65, 52), (72, 54))
SPLIT_STEPS = (73, 75, 77, 79, 80, 81, 82)
WIDE_AT = {76: ((0, (0, 1)),), 78: ((1, (0, 1)),), 80: ((2, (0, 1)), (0, (2, 3))), 81: ((1, (2, 3)),),
           82: ((3, (0, 1)), (2, (2, 3))), 83: ((3, (2, 3)),)}

MASK_W = (QT - 1) * P + SEQ
C_IDENT, C_MASK = 0, P
C_COSA = C_MASK + MASK_W
C_SINA = C_COSA + QT * HEAD_DIM
C_COSB = C_SINA + QT * HEAD_DIM
C_SINB = C_COSB + QT * HEAD_DIM
C_W = C_SINB + QT * HEAD_DIM


def shape_constants():
    c = np.zeros((P, C_W), np.float32)
    c[:, C_IDENT:C_IDENT + P] = np.eye(P, dtype=np.float32)
    dist = np.arange(P)[:, None] - np.arange(MASK_W)[None, :] + (QT - 1) * P
    count = sum(((dist % dil == 0) & (abs(dist) <= dil * (window // (2 * dil)))).astype(np.int64)
                for window, dil in DILATED_PATTERNS)
    c[:, C_MASK:C_MASK + MASK_W] = np.where(count > 0, np.log(np.maximum(count, 1)) / SCALE, NEG_BIG)

    def angles(pos, dim):
        inv = 1.0 / (np.float32(ROPE_THETA) ** (np.arange(0, dim, 2, dtype=np.float32) / np.float32(dim)))
        a = pos.astype(np.float32)[:, None] * inv.astype(np.float32)[None, :]
        a = np.concatenate([a, a], -1)
        sign = np.where(np.arange(dim) < dim // 2, -1.0, 1.0)
        return np.cos(a), np.sin(a) * sign

    pos = np.arange(SEQ)
    cos_a, sin_a = angles(pos, HEAD_DIM)
    rows, cols = angles(pos // GRID_W, HEAD_DIM // 2), angles(pos % GRID_W, HEAD_DIM // 2)
    cos_b, sin_b = (np.concatenate([r, k], -1) for r, k in zip(rows, cols))
    for at, table in ((C_COSA, cos_a), (C_SINA, sin_a), (C_COSB, cos_b), (C_SINB, sin_b)):
        c[:, at:at + QT * HEAD_DIM] = table.reshape(QT, P, HEAD_DIM).transpose(1, 0, 2).reshape(P, -1)
    return c


def head_columns(j):
    if j < N_HEADS_B:
        kv = j // (N_HEADS_B // N_KV_B)
        return (COL["qb"] + 64 * j, COL["kb"] + 64 * kv, COL["vb"] + 64 * kv,
                (WIDTH_A + 64 * j) // P, kv, False)
    h = j - N_HEADS_B
    return (COL["qa"] + 64 * h, COL["ka"] + 64 * h, COL["va"] + 64 * h, 64 * h // P, N_KV_B + h, True)


def head_rows(j):
    return slice(HEAD_DIM * (j % 2), HEAD_DIM * (j % 2 + 1))


def build(nc, x_prompt, x_sample, w_in, w_out, q_norm, k_norm, ln_g, ln_b, consts, y_prompt, y_sample):
    ctx = ExitStack()
    with ctx:
        def sb(name, shape, dt=F32):
            return ctx.enter_context(nc.sbuf_tensor(name, shape, dt))

        def sem(name):
            return ctx.enter_context(nc.semaphore(name))

        t_hi = sb("t_hi", [P, KT, TOK], F32R)
        t_lo = sb("t_lo", [P, KT, TOK], F32R)
        w_hi = sb("w_hi", [P, RING, 2, CW], F32R)
        w_lo = sb("w_lo", [P, RING, 2, CW], F32R)
        q_st = sb("q_st", [P, 2, TOK], F32R)
        k_hi = sb("k_hi", [P, 2, TOK], F32R)
        k_lo = sb("k_lo", [P, 2, TOK], F32R)
        v_st = sb("v_st", [P, 2, TILES, 2 * HEAD_DIM], F32R)
        k_two = sb("k_two", [P, TILES, 2 * HEAD_DIM])
        p_hi = sb("p_hi", [P, 2, 2, SEQ], F32R)
        p_lo = sb("p_lo", [P, 2, 2, SEQ], F32R)
        h = sb("h", [P, TILES, H_WIDTH])
        mix_t = sb("mix_t", [P, KT, TOK])
        raw = sb("raw", [P, RAW, 2, CW])
        cst = sb("cst", [P, C_W])
        cos_k = sb("cos_k", [P, QT, HEAD_DIM])
        sin_k = sb("sin_k", [P, QT, HEAD_DIM])
        tmp_c = sb("tmp_c", [P, 2, CW])
        tmp_s = sb("tmp_s", [P, 2, CW])
        prob = sb("prob", [P, PRING, SEQ])
        tanh = sb("tanh", [P, SEQ])
        o_lo = sb("o_lo", [P, 2 * P])
        nmax = sb("nmax", [P, 2, TILES])
        den = sb("den", [P, 2, TILES])
        norms = prob[:, 0, 0:2 * HEAD_DIM].rearrange("p (w d) -> p w d", w=2)
        ssq = sb("ssq", [P, 2, TILES, HPC])
        squares = tanh[:].rearrange("p (n c) -> p n c", c=CW)
        rstd = sb("rstd", [P, 2, TILES * HPC])
        half = sb("half", [P, TILES * HPC])
        zero = sb("zero", [P, 1])
        scr = sb("scr", [P, TILES * HPC])

        ident = cst[:, C_IDENT:C_IDENT + P]
        cos_b = cst[:, C_COSB:C_COSB + QT * HEAD_DIM].rearrange("p (t d) -> p t d", d=HEAD_DIM)
        sin_b = cst[:, C_SINB:C_SINB + QT * HEAD_DIM].rearrange("p (t d) -> p t d", d=HEAD_DIM)
        stats = cst[:, C_COSB:C_COSB + TILES * OUT_CHUNKS * 6] \
            .rearrange("p (t c s) -> p t c s", c=OUT_CHUNKS, s=6)
        mv = cst[:, C_SINB:C_SINB + TILES * 2].rearrange("p (t s) -> p t s", s=2)
        lnr = cst[:, C_SINB + TILES * 2:C_SINB + TILES * 6].rearrange("p (t s) -> p t s", s=4)

        def table(at, t):
            k = t if t < QT else t - QT
            return cst[:, at + k * HEAD_DIM:at + (k + 1) * HEAD_DIM]

        bank = [ctx.enter_context(nc.psum_tensor(f"bank{i}", [P, 512], F32)) for i in range(8)]
        acc, s_ps, pt_ps, o_ps, t_ps = bank[0:2], bank[2:4], bank[4:6], bank[6], bank[7]

        x_loaded = [sem(f"x_loaded{t}") for t in range(TILES)]
        x_half_loaded, ident_loaded, consts_loaded = sem("x_half_loaded"), sem("ident_loaded"), sem("consts_loaded")
        norms_loaded = sem("norms_loaded")
        raw_loaded = [sem(f"raw_loaded{i}") for i in range(SLICES)]
        hi_done = sem("w_hi_done")
        w_lo_pool, w_lo_dve = sem("w_lo_pool"), sem("w_lo_dve")
        tables_ready = sem("tables_ready")
        pool_consts = sem("pool_consts")
        xt_written, xt_hi, xt_lo = sem("xt_written"), sem("xt_hi"), sem("xt_lo")
        acc_ready = sem("acc_ready")
        act_evacuated, dve_evacuated = sem("act_evacuated"), sem("dve_evacuated")
        tanh_done = sem("tanh_done")
        products_ready, rope_added = sem("products_ready"), sem("rope_added")
        squared, summed, rstd_ready, normed = sem("squared"), sem("summed"), sem("rstd_ready"), sem("normed")
        pool_step, dve_step = sem("pool_step"), sem("dve_step")
        t_written, t_hi_done, t_lo_done = sem("t_written"), sem("t_hi_done"), sem("t_lo_done")
        v_split, keys_doubled = sem("v_split"), sem("keys_doubled")
        s_ready, s_masked = sem("s_ready"), sem("s_masked")
        exp_done = sem("exp_done")
        pt_ready, pt_hi_done, pt_lo_done = sem("pt_ready"), sem("pt_hi_done"), sem("pt_lo_done")
        pv_done, low_copied = sem("pv_done"), sem("low_copied")
        den_inverted, scaled, mixed = sem("den_inverted"), sem("scaled"), sem("mixed")
        mix_hi, mix_lo_pool, mix_lo_dve = sem("mix_hi"), sem("mix_lo_pool"), sem("mix_lo_dve")
        slice_used = sem("slice_used")
        xres_loaded = sem("xres_loaded")
        ln_loaded = sem("ln_loaded")
        stats_ready, ln_rstd, ln_normed, ln_scaled, y_ready = (
            sem("stats_ready"), sem("ln_rstd"), sem("ln_normed"), sem("ln_scaled"), sem("y_ready"))
        stored = sem("stored")

        block = ctx.enter_context(nc.Block())

        AHEAD = (IN_CHUNKS + 1) * SLICES + RAW

        def kind_of(c):
            return KIND[ORDER[c]] if c < IN_CHUNKS else None

        parts = [2 * (CW // P) if kind_of(c) == GATE else TILES for c in range(CHUNKS)]
        items = [(c, n) for c in range(CHUNKS - 2) for n in range(parts[c])]
        items += [(c, n) for n in range(TILES) for c in (CHUNKS - 2, CHUNKS - 1)]
        index = {item: i for i, item in enumerate(items)}
        IN_ITEMS = index[(IN_CHUNKS, 0)]
        evac = []
        n_act = n_dve = n_rot = 0
        for c, n in items:
            n_rot += kind_of(c) in (NORM, ROPE)
            if kind_of(c) in (NORM, VALUE):
                n_act += 1
                evac.append((act_evacuated, n_act))
            elif kind_of(c) == ROPE:
                evac.append((products_ready, n_rot))
            else:
                n_dve += 1
                evac.append((dve_evacuated, n_dve))
        gates = [item for item in items if kind_of(item[0]) == GATE]
        ropes = [item for item in items if kind_of(item[0]) in (NORM, ROPE)]
        norm_chunks = [c for c in range(IN_CHUNKS) if kind_of(c) == NORM]
        beside = [item for item in items if ALONE <= item[0] < IN_CHUNKS]

        own_kv = [j == 0 or head_columns(j)[4] != head_columns(j - 1)[4] for j in range(HEADS)]

        def staging(j):
            return [("q", j)] + ([("k", j)] if own_kv[j] else []) + [("r", j)]

        def items_before(u):
            for (u0, n0), (u1, n1) in zip(BESIDE, BESIDE[1:]):
                if u <= u1:
                    return n0 + (u - u0) * (n1 - n0) // (u1 - u0)
            return len(beside)

        def items_at(u):
            return beside[items_before(u):items_before(u + 1)]

        first_items = beside[items_before(0) - len(staging(0)):items_before(0)]
        alone = [item for item in items if 1 <= item[0] < ALONE] + beside[:items_before(0) - len(staging(0))]
        assert BESIDE[-1][1] == len(beside)

        WIDE = 4

        def accumulator(i):
            return s_ps[i - IN_ITEMS - 2] if IN_ITEMS + 2 <= i < IN_ITEMS + WIDE else acc[i % 2]

        def last_in_bank(i):
            if i < 2 or accumulator(i) is not acc[i % 2]:
                return None
            return i - WIDE if IN_ITEMS + WIDE <= i < IN_ITEMS + WIDE + 2 else i - 2

        def chunk_end(list_, w_chunk):
            c = ORDER.index(w_chunk)
            return sum(1 for item in list_ if item[0] <= c)

        def copies_through(w_chunk):
            c = ORDER.index(w_chunk)
            return evac[index[(c, parts[c] - 1)]][1]

        def heads_chunk(j, what):
            if j < N_HEADS_B:
                return {"q": 8 + j // HPC, "k": KEYS_B, "v": KEYS_B}[what]
            return {"q": 0, "k": 2, "v": 4}[what] + (j - N_HEADS_B) // HPC

        def late_tiles(c, n):
            return range(n * TILES // parts[c], (n + 1) * TILES // parts[c])

        def slices_at(c, n):
            at = {1: [0], 3: [1], 5: [2, 3]} if parts[c] == TILES else {0: [0], 2: [1], 3: [2, 3]}
            return [(c + 1) * SLICES + s for s in at.get(n, [])]

        def raw_slot(g):
            return prob[:, g, :].rearrange("p (k c) -> p k c", k=2) if RAW <= g < SLICES else raw[:, g % RAW, :, :]

        def raw_arrival(g):
            return (raw_loaded[g], 16) if g < SLICES else (raw_loaded[g % RAW], 16 * (1 + (g - SLICES) // RAW + 1))

        def ring_place(g):
            c = g // SLICES
            return g if c < CHUNKS - 2 else None if c == CHUNKS - 2 else g - SLICES

        def w_slot(g):
            turn = ring_place(g)
            if turn is not None:
                return w_hi[:, turn % RING, :, :], w_lo[:, turn % RING, :, :]
            s = g % SLICES
            if s < 3:
                pair, at = (k_hi[:], k_lo[:]), s
            else:
                pair, at = (q_st[:], v_st[:].rearrange("p s t d -> p s (t d)")), 0
            return [a.rearrange("p s t -> p (s t)")[:, 2 * CW * at:2 * CW * (at + 1)].rearrange("p (k c) -> p k c", k=2)
                    for a in pair]

        def on_dve(g):
            return g % SLICES > 0 and g // SLICES in DVE_LOW_CHUNKS

        def low_taken(g):
            return (w_lo_dve if on_dve(g) else w_lo_pool), sum(1 for s in range(g + 1) if on_dve(s) == on_dve(g))

        def chunk_source(c):
            if c < IN_CHUNKS:
                w, at, order = w_in, ORDER[c] * CW, list(range(KT))
            else:
                w, at, order = w_out, (c - IN_CHUNKS) * CW, split_order
            return w[:, at:at + CW].rearrange("(k p) n -> p k n", p=P), order

        def x_rows(t):
            return x_prompt[t * P:(t + 1) * P, :] if t < QT else x_sample[(t - QT) * P:(t - QT + 1) * P, :]

        def y_rows(t):
            return y_prompt[t * P:(t + 1) * P, :] if t < QT else y_sample[(t - QT) * P:(t - QT + 1) * P, :]

        steps = {u: [] for u in range(STEPS)}
        for j in range(HEADS - 1):
            for n, b in enumerate(staging(j + 1)):
                steps[UNITS * j + (0, 2, 3)[n]].append(b)
        first = staging(0)
        t_count = {}
        for b in first + [b for u in range(STEPS) for b in steps[u]]:
            t_count[b] = len(t_count)
        staged = [t_count[staging(j)[-1]] + 1 for j in range(HEADS)]

        split_order = [*range(N_HEADS_A // 2, KT), *range(N_HEADS_A // 2)]
        split_at = dict(zip(SPLIT_STEPS, split_order))

        def group_of(u):
            j, k = divmod(u, UNITS)
            return GROUPS * j + k // 2

        def groups_at(u):
            v = u - LAG - 1
            return [group_of(v)] if 0 <= v < NU and (v == NU - 1 or group_of(v + 1) != group_of(v)) else []

        def mixed_through(j):
            return GROUPS * (j + 1)

        def transposed_at(u):
            return group_of(u) % 2, u % UNITS % 2

        def norm_heads(c):
            return N_KV_B if ORDER[c] == KEYS_B else HPC

        @block.sync
        def _(sp):
            def load_slice(g):
                if g >= SLICES:
                    sp.wait_ge(*low_taken(g - RAW if g >= SLICES + RAW else g - SLICES))
                c, s = divmod(g, SLICES)
                source, order = chunk_source(c)
                k = order[2 * s]
                sp.dma_start(raw_slot(g), source[:, k:k + 2, :]).then_inc(raw_arrival(g)[0], 16)

            sp.dma_start(h[:, 0, 0:D_MODEL // 2], x_rows(0)[:, 0:D_MODEL // 2]).then_inc(x_half_loaded, 16)
            sp.dma_start(h[:, 0, D_MODEL // 2:D_MODEL], x_rows(0)[:, D_MODEL // 2:D_MODEL]).then_inc(x_loaded[0], 16)
            for t in range(1, TILES):
                if t == 1:
                    for g in range(SLICES):
                        load_slice(g)
                sp.dma_start(h[:, t, 0:D_MODEL], x_rows(t)).then_inc(x_loaded[t], 16)
                if t == CONSTS_AFTER:
                    sp.dma_start(cst[:, P:C_W], consts[:, P:C_W]).then_inc(consts_loaded, 16)
            for g in range(SLICES, AHEAD):
                load_slice(g)
            sp.wait_ge(t_written, staged[HEADS - 1])
            sp.wait_ge(v_split, HEADS // 2 + N_KV_B)
            for t in range(TILES):
                sp.dma_start(h[:, t, 0:D_MODEL], x_rows(t)).then_inc(xres_loaded, 16)
            for n, src in enumerate((ln_g, ln_b)):
                for k in range(2):
                    sp.dma_start(h[:, 2 * n + k, 2 * WIDTH_A:3 * WIDTH_A],
                                 src[None, k * 512:(k + 1) * 512].to_broadcast([P, 512])).then_inc(ln_loaded, 16)
            for g in range(AHEAD, CHUNKS * SLICES):
                load_slice(g)
            for t in range(TILES):
                for n in range(2):
                    sp.wait_ge(y_ready, 2 * t + n + 1)
                    cols = slice(n * 512, (n + 1) * 512)
                    sp.dma_start(y_rows(t)[:, cols], h[:, t, cols]).then_inc(stored, 16)
            sp.wait_ge(stored, 2 * 16 * TILES)

        @block.tensor
        def _(pe):
            def transpose_batch(dst, pieces):
                for n, src in enumerate(pieces):
                    ins = nc.tensor.transpose(dst[0:src.shape[-1], n * P:(n + 1) * P], src, ident)
                return ins

            def x_transposes(t):
                for b in range(2):
                    pe.wait_ge(x_half_loaded if t == b == 0 else x_loaded[t], 16)
                    i = 2 * t + b
                    if i >= 2:
                        pe.wait_ge(xt_lo, i - 1)
                    transpose_batch(pt_ps[i % 2], [h[:, t, (4 * b + n) * P:(4 * b + n + 1) * P] for n in range(4)]) \
                        .then_inc(xt_written, 1)

            def accumulate(c, n, m):
                i = index[(c, n)]
                k = chunk_source(c)[1][m]
                g = c * SLICES + m // 2
                out = accumulator(i)
                if m == 0 and last_in_bank(i) is not None:
                    pe.wait_ge(*evac[last_in_bank(i)])
                if n == 0 and m % 2 == 0:
                    pe.wait_ge(*low_taken(g))
                if c == IN_CHUNKS and n == 0:
                    if k >= N_HEADS_A // 2:
                        pe.wait_ge(mix_lo_pool, m + 1)
                    else:
                        pe.wait_ge(mix_lo_dve, m + 1 - N_HEADS_B // 2)
                w_h, w_l = (a[:, m % 2, :] for a in w_slot(g))
                if kind_of(c) == GATE:
                    e, cols = n // 2, slice(0, SEQ) if n % 2 == 0 else slice(SEQ, TOK)
                    a_hi, a_lo = w_h[:, e * P:(e + 1) * P], w_l[:, e * P:(e + 1) * P]
                    b_hi, b_lo = t_hi[:, k, cols], t_lo[:, k, cols]
                    out = out[:, 0:cols.stop - cols.start]
                else:
                    a_hi, a_lo = t_hi[:, k, n * P:(n + 1) * P], t_lo[:, k, n * P:(n + 1) * P]
                    b_hi, b_lo = w_h, w_l
                    out = out[:, 0:CW]
                nc.tensor.matmul(out, a_lo, b_hi, start=(m == 0), stop=False)
                nc.tensor.matmul(out, a_hi, b_lo, start=False, stop=False)
                ins = nc.tensor.matmul(out, a_hi, b_hi, start=False, stop=(m == KT - 1))
                if m == KT - 1:
                    ins.then_inc(acc_ready, 1)
                elif n == parts[c] - 1 and m % 2 == 1:
                    ins.then_inc(slice_used, 1)

            def project(c, n):
                for m in range(KT):
                    accumulate(c, n, m)

            def wide_tile(m, tiles=range(WIDE)):
                for n in tiles:
                    if m == 0 and n == 2:
                        pe.wait_ge(s_masked, NU)
                    accumulate(IN_CHUNKS, n, m)

            def t_batch(b):
                n = t_count[b]
                if n:
                    pe.wait_ge(t_lo_done, n)
                qc, kc, _, _, kv, _ = head_columns(b[1])
                if b[0] == "q":
                    pe.wait_ge(rope_added, chunk_end(ropes, heads_chunk(b[1], "q")))
                    pieces = [h[:, t, qc:qc + HEAD_DIM] for t in range(QT)]
                elif b[0] == "k":
                    pe.wait_ge(keys_doubled, kv + 1)
                    pieces = [k_two[:, t, :] for t in range(QT)]
                else:
                    pieces = [h[:, QT + t, qc:qc + HEAD_DIM] for t in range(ST)]
                    if own_kv[b[1]]:
                        pieces += [k_two[:, QT + t, :] for t in range(ST)]
                transpose_batch(t_ps, pieces).then_inc(t_written, 1)

            def scores(u):
                j, k = divmod(u, UNITS)
                kv = head_columns(j)[4]
                if k == 0:
                    pe.wait_ge(t_lo_done, staged[j])
                if u >= 2:
                    pe.wait_ge(s_masked, u - 1)
                out = s_ps[u % 2]
                q = q_st[:, j % 2, :]
                if k < QT:
                    nc.tensor.matmul(out[:], q[:, k * P:(k + 1) * P], k_lo[:, kv % 2, 0:SEQ], start=True, stop=False)
                    ins = nc.tensor.matmul(out[:], q[:, k * P:(k + 1) * P], k_hi[:, kv % 2, 0:SEQ],
                                           start=False, stop=True)
                else:
                    for t in range(ST):
                        o = out[:, t * DEC_SEQ:(t + 1) * DEC_SEQ]
                        lhs = q[:, SEQ + t * P:SEQ + (t + 1) * P]
                        nc.tensor.matmul(o, lhs, k_lo[:, kv % 2, SEQ:TOK], start=True, stop=False)
                        ins = nc.tensor.matmul(o, lhs, k_hi[:, kv % 2, SEQ:TOK], start=False, stop=True)
                ins.then_inc(s_ready, 1)

            def prob_transposes(u):
                pe.wait_ge(scaled, u + 1)
                if u >= 2:
                    pe.wait_ge(pt_lo_done, u - 1)
                transpose_batch(pt_ps[u % 2], [prob[:, u % PRING, n * P:(n + 1) * P] for n in range(4)]) \
                    .then_inc(pt_ready, 1)

            def values(g):
                j, k = divmod(g, GROUPS)
                kv = head_columns(j)[4]
                if k == 0:
                    pe.wait_ge(v_split, kv + 1)
                if g:
                    pe.wait_ge(mixed, g)
                u = UNITS * j + 2 * k
                sample = k == GROUPS - 1
                pe.wait_ge(pt_lo_done, u + (1 if sample else 2))
                base, keys = (QT, ST) if sample else (0, QT)
                o = o_ps[:, 0:2 * P].rearrange("p (t q) -> p t q", t=2)
                for n in range(keys):
                    if sample:
                        hi, lo = (a[:, g % 2, 0, :].rearrange("p (t n q) -> p t n q", n=ST, q=P)[:, :, n, :]
                                  for a in (p_hi, p_lo))
                    else:
                        hi, lo = (a[:, g % 2, :, n * P:(n + 1) * P] for a in (p_hi, p_lo))
                    v = v_st[:, kv % 2, base + n, :]
                    passes = [(o, v, hi), (o[0:HEAD_DIM], v[:, 0:HEAD_DIM], lo)]
                    last = n == keys - 1
                    for out, lhs, rhs in passes[::-1] if last else passes:
                        ins = nc.tensor.matmul(out, lhs, rhs, start=(n == 0 and rhs is hi), stop=(last and rhs is hi))
                ins.then_inc(pv_done, 1)

            pe.wait_ge(ident_loaded, 16)
            x_transposes(0)
            for t in range(TILES):
                if t + 1 < TILES:
                    x_transposes(t + 1)
                pe.wait_ge(xt_lo, 2 * t + 2)
                project(0, t)
            for item in alone:
                project(*item)
            for b, item in zip(first, first_items):
                t_batch(b)
                project(*item)
            for u in range(STEPS):
                if u < NU:
                    scores(u)
                for m, tiles in WIDE_AT.get(u, ()):
                    wide_tile(m, tiles)
                for b in steps[u]:
                    t_batch(b)
                if LAG <= u < NU + LAG:
                    prob_transposes(u - LAG)
                for item in items_at(u):
                    project(*item)
                for g in groups_at(u):
                    values(g)
            for m in range(KT // 2, KT):
                wide_tile(m)
            for item in items[IN_ITEMS + WIDE:]:
                project(*item)

        def t_destination(b):
            j = b[1]
            kv = head_columns(j)[4]
            if b[0] == "q":
                return [(0, SEQ, q_st[0:HEAD_DIM, j % 2, 0:SEQ])]
            if b[0] == "k":
                return [(0, SEQ, k_hi[:, kv % 2, 0:SEQ])]
            out = [(0, DEC_SEQ, q_st[0:HEAD_DIM, j % 2, SEQ:TOK])]
            if own_kv[j]:
                out.append((DEC_SEQ, 2 * DEC_SEQ, k_hi[:, kv % 2, SEQ:TOK]))
            return out

        @block.scalar
        def _(act):
            act.dma_start(cst[:, 0:P], consts[:, 0:P]).then_inc(ident_loaded, 16)
            act.dma_start(norms[:, 0, :], q_norm[None, :].to_broadcast([P, HEAD_DIM])).then_inc(norms_loaded, 16)
            act.dma_start(norms[:, 1, :], k_norm[None, :].to_broadcast([P, HEAD_DIM])).then_inc(norms_loaded, 16)

            def weights_high(g):
                act.wait_ge(*raw_arrival(g))
                turn = ring_place(g)
                if turn is None:
                    act.wait_ge(pv_done, GROUPS * HEADS)
                elif turn >= RING:
                    c, s = divmod(turn - RING, SLICES)
                    if s < SLICES - 1:
                        act.wait_ge(slice_used, (SLICES - 1) * c + s + 1)
                    else:
                        act.wait_ge(acc_ready, index[(c, parts[c] - 1)] + 1)
                nc.scalar.activation(w_slot(g)[0], raw_slot(g), ACT.Copy).then_inc(hi_done, 1)

            def x_high(t):
                for b in range(2):
                    i = 2 * t + b
                    act.wait_ge(xt_written, i + 1)
                    nc.scalar.activation(t_hi[:, 4 * b:4 * b + 4, t * P:(t + 1) * P],
                                         pt_ps[i % 2][:].rearrange("p (n q) -> p n q", n=4), ACT.Copy) \
                        .then_inc(xt_hi, 1)

            def evacuate(c, n):
                i = index[(c, n)]
                kind = kind_of(c)
                if kind == ROPE:
                    return
                act.wait_ge(acc_ready, i + 1)
                if kind == GATE:
                    m = gates.index((c, n))
                    w = SEQ if n % 2 == 0 else DEC_SEQ
                    if m >= 1:
                        act.wait_ge(dve_evacuated, m)
                    if n == 0:
                        act.wait_ge(summed, TILES * sum(1 for d in norm_chunks if d < c))
                    nc.scalar.activation(tanh[:, 0:w], acc[i % 2][:, 0:w], ACT.Tanh, scale=0.5) \
                        .then_inc(tanh_done, 1)
                else:
                    at = HOME[ORDER[c]]
                    nc.scalar.activation(h[:, n, at:at + CW], acc[i % 2][:, 0:CW], ACT.Copy).then_inc(act_evacuated, 1)

            def t_high(b):
                n = t_count[b]
                act.wait_ge(t_written, n + 1)
                if b[0] in ("q", "k"):
                    j = b[1]
                    if j >= 2:
                        act.wait_ge(s_ready, UNITS * (j - 1))
                for a, z, dst in t_destination(b):
                    ins = nc.scalar.activation(dst, t_ps[0:dst.shape[0], a:z], ACT.Copy)
                ins.then_inc(t_hi_done, 1)

            def exps(u):
                j, k = divmod(u, UNITS)
                act.wait_ge(s_masked, u + 1)
                rows = [(k, 0, SEQ)] if k < QT else [(QT + t, t * DEC_SEQ, (t + 1) * DEC_SEQ) for t in range(ST)]
                for t, a, z in rows:
                    s = prob[:, u % PRING, a:z]
                    ins = nc.scalar.activation(s, s, ACT.Exp, scale=-1.0, bias=nmax[:, j % 2, t:t + 1],
                                               accum_out=den[:, j % 2, t:t + 1])
                ins.then_inc(exp_done, 1)

            def prob_high(u):
                act.wait_ge(pt_ready, u + 1)
                if group_of(u) >= 2:
                    act.wait_ge(pv_done, group_of(u) - 1)
                slot, place = transposed_at(u)
                nc.scalar.activation(p_hi[:, slot, place, :], pt_ps[u % 2][:], ACT.Copy).then_inc(pt_hi_done, 1)

            def copy_low(g):
                act.wait_ge(pv_done, g + 1)
                rows = head_rows(g // GROUPS)
                nc.scalar.activation(o_lo[rows, :], o_ps[HEAD_DIM:P, 0:2 * P], ACT.Copy).then_inc(low_copied, 1)

            def split_mixed(n):
                e = split_order[n]
                if n == 0:
                    act.wait_ge(acc_ready, IN_ITEMS)
                j = 2 * e - N_HEADS_A if e >= N_HEADS_A // 2 else 2 * e + N_HEADS_B
                act.wait_ge(mixed, mixed_through(j + 1))
                nc.scalar.activation(t_hi[:, e, :], mix_t[:, e, :], ACT.Copy).then_inc(mix_hi, 1)

            for g in range(2):
                weights_high(g)
            x_high(0)
            for g in range(2, 4):
                weights_high(g)
            for t in range(1, TILES):
                x_high(t)
                for g in slices_at(0, t):
                    weights_high(g)
                evacuate(0, t - 1)
            evacuate(0, TILES - 1)
            for c, n in alone:
                for g in slices_at(c, n):
                    weights_high(g)
                evacuate(c, n)
            for b, (c, n) in zip(first, first_items):
                t_high(b)
                for g in slices_at(c, n):
                    weights_high(g)
                evacuate(c, n)
            for u in range(STEPS):
                for b in steps[u]:
                    t_high(b)
                if LAG <= u < NU + LAG:
                    prob_high(u - LAG)
                if u < NU:
                    exps(u)
                for c, n in items_at(u):
                    for g in slices_at(c, n):
                        weights_high(g)
                    evacuate(c, n)
                for g in groups_at(u):
                    copy_low(g)
                if u in split_at:
                    split_mixed(split_order.index(split_at[u]))
            split_mixed(KT - 1)
            for g in range((IN_CHUNKS + 1) * SLICES, CHUNKS * SLICES):
                weights_high(g)
            for t in range(TILES):
                act.wait_ge(ln_rstd, t + 1)
                for half_at in (512, 0):
                    r = h[:, t, half_at:half_at + 512]
                    nc.scalar.activation(r, r, ACT.Identity, scale=lnr[:, t, 0:1], bias=lnr[:, t, 1:2]) \
                        .then_inc(ln_normed, 1)

        @block.vector
        def _(dve):
            links = [0]

            def after(ins):
                links[0] += 1
                ins.then_inc(dve_step, 1)
                dve.wait_ge(dve_step, links[0])

            def swap_halves(out, in_, tab, heads, block_w):
                n = HEAD_DIM // block_w
                w = block_w // 2
                for a, b in ((0, w), (w, 0)):
                    for k in range(n):
                        o = out.rearrange("p (m d) -> p m d", d=HEAD_DIM)[:, :, k * block_w + a:k * block_w + a + w]
                        i = in_.rearrange("p (m d) -> p m d", d=HEAD_DIM)[:, :, k * block_w + b:k * block_w + b + w]
                        tt = tab[:, None, k * block_w + a:k * block_w + a + w].to_broadcast([P, heads, w])
                        ins = nc.vector.tensor_tensor(o, i, tt, ALU.mult)
                return ins

            def heads_of(ap):
                return ap.rearrange("p (m d) -> p m d", d=HEAD_DIM)

            def x_low(t):
                for b in range(2):
                    i = 2 * t + b
                    dve.wait_ge(xt_hi, i + 1)
                    at = t_hi[:, 4 * b:4 * b + 4, t * P:(t + 1) * P]
                    nc.vector.tensor_tensor(t_lo[:, 4 * b:4 * b + 4, t * P:(t + 1) * P],
                                            pt_ps[i % 2][:].rearrange("p (n q) -> p n q", n=4),
                                            at.bitcast(F32), ALU.subtract).then_inc(xt_lo, 1)

            def rotate(src, cos, sin, heads, block_w, n):
                if n >= 2:
                    dve.wait_ge(rope_added, n - 1)
                nc.vector.tensor_tensor(heads_of(tmp_c[:, n % 2, 0:heads * HEAD_DIM]), heads_of(src),
                                        cos[:, None, :].to_broadcast([P, heads, HEAD_DIM]), ALU.mult)
                ins = swap_halves(tmp_s[:, n % 2, 0:heads * HEAD_DIM], src, sin, heads, block_w)
                ins.then_inc(products_ready, 1)

            def sums(c, t):
                i = norm_chunks.index(c)
                n = i * TILES + t
                dve.wait_ge(squared, n + 1)
                m = norm_heads(c)
                nc.vector.reduce_sum(ssq[:, i % 2, t, 0:m], heads_of(squares[:, n % 2, 0:m * HEAD_DIM]), axis=AX.X) \
                    .then_inc(summed, 1)

            def norm_and_rotate(c, t):
                cos, sin = (cos_k, sin_k) if ORDER[c] == KEYS_B else (cos_b, sin_b)
                m = norm_heads(c)
                i = norm_chunks.index(c)
                dve.wait_ge(rstd_ready, i + 1)
                at = HOME[ORDER[c]]
                src = h[:, t, at:at + m * HEAD_DIM]
                k = t if t < QT else t - QT
                r = rstd[:, i % 2, t * HPC:t * HPC + m]
                after(nc.vector.tensor_tensor(heads_of(src), heads_of(src),
                                              r[:, :, None].to_broadcast([P, m, HEAD_DIM]), ALU.mult))
                rotate(src, cos[:, k, :], sin[:, k, :], m, HEAD_DIM // 2, ropes.index((c, t)))

            def evacuate(c, n):
                i = index[(c, n)]
                if kind_of(c) == GATE:
                    m = gates.index((c, n))
                    cols = slice(0, SEQ) if n % 2 == 0 else slice(SEQ, TOK)
                    w = cols.stop - cols.start
                    dve.wait_ge(tanh_done, m + 1)
                    nc.vector.scalar_tensor_tensor(
                        out=mix_t[:, HOME[ORDER[c]] + n // 2, cols], in0=tanh[:, 0:w], scalar=1.0,
                        in1=acc[i % 2][:, 0:w], op0=ALU.add, op1=ALU.mult).then_inc(dve_evacuated, 1)
                elif kind_of(c) == ROPE:
                    dve.wait_ge(acc_ready, i + 1)
                    rotate(acc[i % 2][:, 0:CW], table(C_COSA, n), table(C_SINA, n), HPC, HEAD_DIM,
                           ropes.index((c, n)))

            def mask_max(u):
                j, k = divmod(u, UNITS)
                is_a = head_columns(j)[5]
                dve.wait_ge(s_ready, u + 1)
                if u >= PRING:
                    dve.wait_ge(pt_ready, u - PRING + 1)
                rows = [(k, 0, SEQ)] if k < QT else [(QT + t, t * DEC_SEQ, (t + 1) * DEC_SEQ) for t in range(ST)]
                for t, a, z in rows:
                    if is_a:
                        m0 = C_MASK + (QT - 1 - (t if t < QT else t - QT)) * P
                        mask = cst[:, m0:m0 + z - a]
                    else:
                        mask = zero[:].to_broadcast([P, z - a])
                    ins = nc.vector.tensor_tensor_reduce(
                        out=prob[:, u % PRING, a:z], in0=s_ps[u % 2][:, a:z], in1=mask, scale=-SCALE,
                        scalar=-NEG_BIG, op0=ALU.add, op1=ALU.min, accum_out=nmax[:, j % 2, t:t + 1])
                ins.then_inc(s_masked, 1)

            def prob_low(u):
                dve.wait_ge(pt_hi_done, u + 1)
                slot, place = transposed_at(u)
                nc.vector.tensor_tensor(p_lo[:, slot, place, :], pt_ps[u % 2][:], p_hi[:, slot, place, :].bitcast(F32),
                                        ALU.subtract).then_inc(pt_lo_done, 1)

            def t_low(b):
                n = t_count[b]
                dve.wait_ge(t_hi_done, n + 1)
                for a, z, dst in t_destination(b):
                    if b[0] == "k" or a:
                        kv = head_columns(b[1])[4]
                        lo = k_lo[:, kv % 2, 0:SEQ] if b[0] == "k" else k_lo[:, kv % 2, SEQ:TOK]
                        ins = nc.vector.tensor_tensor(lo, t_ps[:, a:z], dst.bitcast(F32), ALU.subtract)
                    else:
                        low = q_st[HEAD_DIM:P, b[1] % 2, 0:SEQ] if b[0] == "q" else \
                            q_st[HEAD_DIM:P, b[1] % 2, SEQ:TOK]
                        ins = nc.vector.tensor_tensor(low, t_ps[0:HEAD_DIM, a:z], dst.bitcast(F32), ALU.subtract)
                ins.then_inc(t_lo_done, 1)

            def invert(u):
                j, k = divmod(u, UNITS)
                t = slice(k, k + 1) if k < QT else slice(QT, TILES)
                dve.wait_ge(exp_done, u + 1)
                nc.vector.reciprocal(den[:, j % 2, t], den[:, j % 2, t]).then_inc(den_inverted, 1)

            def mix(g):
                j, k = divmod(g, GROUPS)
                rows = head_rows(j)
                dve.wait_ge(low_copied, g + 1)
                o = o_lo[rows, :]
                after(nc.vector.tensor_tensor(o, o_ps[0:HEAD_DIM, 0:2 * P], o, ALU.add))
                gate = mix_t[rows, head_columns(j)[3], 2 * P * k:2 * P * (k + 1)]
                nc.vector.tensor_tensor(gate, o, gate, ALU.mult).then_inc(mixed, 1)

            def weights_low(g):
                if on_dve(g):
                    dve.wait_ge(hi_done, g + 1)
                    nc.vector.tensor_tensor(w_slot(g)[1], raw_slot(g), w_slot(g)[0].bitcast(F32),
                                            ALU.subtract).then_inc(w_lo_dve, 1)

            def mixed_low(n):
                e = split_order[n]
                dve.wait_ge(mix_hi, n + 1)
                nc.vector.tensor_tensor(t_lo[:, e, :], mix_t[:, e, :], t_hi[:, e, :].bitcast(F32), ALU.subtract) \
                    .then_inc(mix_lo_dve, 1)

            nc.vector.memset(zero[:], 0.0)
            nc.vector.memset(half[:], -0.5).then_inc(pool_consts, 1)
            x_low(0)
            for g in range(SLICES):
                weights_low(g)
            dve.wait_ge(consts_loaded, 16)
            dve.wait_ge(norms_loaded, 32)
            for w, cos, sin in ((1, cos_k[:], sin_k[:]), (0, cos_b, sin_b)):
                g = norms[:, w, :]
                nc.vector.tensor_tensor(cos, cos_b, g[:, None, :].to_broadcast([P, QT, HEAD_DIM]), ALU.mult)
                q = HEAD_DIM // 4
                for k in range(4):
                    o = k ^ 1
                    nc.vector.tensor_tensor(sin[:, :, k * q:(k + 1) * q], sin_b[:, :, k * q:(k + 1) * q],
                                            g[:, None, o * q:(o + 1) * q].to_broadcast([P, QT, q]), ALU.mult) \
                        .then_inc(tables_ready, 1)
                dve.wait_ge(tables_ready, 4 if w else 8)
            for t in range(1, TILES):
                x_low(t)
                for g in slices_at(0, t):
                    weights_low(g)
                sums(0, t - 1)
            sums(0, TILES - 1)

            def after_projection(c, n):
                for g in slices_at(c, n):
                    weights_low(g)
                if kind_of(c) == NORM:
                    sums(c, n)
                if kind_of(c - 1) == NORM:
                    for t in late_tiles(c, n):
                        norm_and_rotate(c - 1, t)
                evacuate(c, n)

            for item in alone:
                after_projection(*item)
            for b, item in zip(first, first_items):
                t_low(b)
                after_projection(*item)
            for u in range(STEPS):
                if 1 <= u < NU + 1:
                    invert(u - 1)
                if u < NU:
                    mask_max(u)
                for b in steps[u]:
                    t_low(b)
                if LAG <= u < NU + LAG:
                    prob_low(u - LAG)
                for item in items_at(u):
                    after_projection(*item)
                for g in groups_at(u):
                    mix(g)
                if split_at.get(u, KT) < N_HEADS_A // 2:
                    mixed_low(split_order.index(split_at[u]))
            mixed_low(KT - 1)

            def residual(c, t):
                i = index[(IN_CHUNKS + c, t)]
                r = h[:, t, c * CW:(c + 1) * CW]
                dve.wait_ge(acc_ready, i + 1)
                after(nc.vector.scalar_tensor_tensor(out=r, in0=r, scalar=ALPHA, in1=accumulator(i)[:, 0:CW],
                                                     op0=ALU.mult, op1=ALU.add))
                nc.vector.bn_stats(stats[:, t, c, :], r).then_inc(dve_evacuated, 1)
                if c == OUT_CHUNKS - 1:
                    dve.wait_ge(*evac[i])
                    nc.vector.bn_aggr(mv[:, t, :], stats[:, t, :, :]).then_inc(stats_ready, 1)

            def affine(t):
                dve.wait_ge(ln_normed, 2 * t + 2)
                r = h[:, t, 0:512]
                after(nc.vector.tensor_tensor(r, r, h[:, 0, 2 * WIDTH_A:3 * WIDTH_A], ALU.mult))
                nc.vector.tensor_tensor(r, r, h[:, 2, 2 * WIDTH_A:3 * WIDTH_A], ALU.add).then_inc(y_ready, 1)
                dve.wait_ge(ln_scaled, t + 1)
                r = h[:, t, 512:D_MODEL]
                nc.vector.tensor_tensor(r, r, h[:, 3, 2 * WIDTH_A:3 * WIDTH_A], ALU.add).then_inc(y_ready, 1)

            dve.wait_ge(xres_loaded, 16 * TILES)
            dve.wait_ge(ln_loaded, 64)
            for c, t in items[IN_ITEMS:]:
                residual(c - IN_CHUNKS, t)
                if c == CHUNKS - 1 and t:
                    affine(t - 1)
            affine(TILES - 1)

        @block.gpsimd
        def _(pool):
            links = [0]

            def after(ins):
                links[0] += 1
                ins.then_inc(pool_step, 1)
                pool.wait_ge(pool_step, links[0])

            def newton(out, v, y):
                after(nc.gpsimd.tensor_tensor(out, y, y, ALU.mult))
                after(nc.gpsimd.tensor_tensor(out, out, v, ALU.mult))
                after(nc.gpsimd.tensor_scalar(out, out, -0.5, 1.5, ALU.mult, ALU.add))
                return nc.gpsimd.tensor_tensor(out, out, y, ALU.mult)

            def weights_low(g):
                if on_dve(g):
                    return
                pool.wait_ge(hi_done, g + 1)
                nc.gpsimd.tensor_tensor(w_slot(g)[1], raw_slot(g), w_slot(g)[0].bitcast(F32),
                                        ALU.subtract).then_inc(w_lo_pool, 1)

            def square(c, t):
                n = norm_chunks.index(c) * TILES + t
                m = norm_heads(c)
                pool.wait_ge(*evac[index[(c, t)]])
                if t == 0:
                    before = sum(1 for g in gates if g[0] < c)
                    if before:
                        pool.wait_ge(dve_evacuated, before)
                if n >= 2:
                    pool.wait_ge(summed, n - 1)
                at = HOME[ORDER[c]]
                src = h[:, t, at:at + m * HEAD_DIM]
                nc.gpsimd.tensor_tensor(squares[:, n % 2, 0:m * HEAD_DIM], src, src, ALU.mult).then_inc(squared, 1)

            def head_views(c, t):
                i, m = norm_chunks.index(c), norm_heads(c)
                flat = slice(t * HPC, t * HPC + m)
                return ssq[:, i % 2, t, 0:m], rstd[:, i % 2, flat], scr[:, flat], half[:, 0:m]

            def head_power(c, t):
                i = norm_chunks.index(c)
                pool.wait_ge(summed, i * TILES + t + 1)
                v, _, y, power = head_views(c, t)
                after(nc.gpsimd.tensor_scalar(v, v, 1.0 / HEAD_DIM, RMS_EPS, ALU.mult, ALU.add))
                after(nc.gpsimd.tensor_tensor(y, v, power, ALU.pow))

            def head_rstd(c):
                i, m = norm_chunks.index(c), norm_heads(c)
                if i >= 2:
                    pool.wait_ge(products_ready, (i - 1) * TILES)
                out, y = (a.rearrange("p (t m) -> p t m", m=HPC)[:, :, 0:m] for a in (rstd[:, i % 2, :], scr[:]))
                newton(out, ssq[:, i % 2, :, 0:m], y).then_inc(rstd_ready, 1)

            def add_rotation(c, t):
                n = ropes.index((c, t))
                m = norm_heads(c)
                pool.wait_ge(products_ready, n + 1)
                if ORDER[c] in (0, 1, 2, 3):
                    pool.wait_ge(xt_written, 2 * TILES)
                at = HOME[ORDER[c]]
                nc.gpsimd.tensor_tensor(h[:, t, at:at + m * HEAD_DIM], tmp_c[:, n % 2, 0:m * HEAD_DIM],
                                        tmp_s[:, n % 2, 0:m * HEAD_DIM], ALU.add).then_inc(rope_added, 1)

            def split_values(j):
                _, _, vc, _, kv, is_a = head_columns(j)
                pool.wait_ge(act_evacuated, copies_through(heads_chunk(j, "v")))
                if kv >= 2:
                    pool.wait_ge(pv_done, GROUPS * (N_HEADS_B // N_KV_B * (kv - 1) if kv <= N_KV_B else
                                                   N_HEADS_B + kv - 1 - N_KV_B))
                hi = v_st[:, kv % 2, :, 0:HEAD_DIM]
                src = h[:, :, vc:vc + HEAD_DIM]
                after(nc.gpsimd.tensor_scalar(hi, src, 1.0, 0.0, ALU.mult, ALU.add))
                nc.gpsimd.tensor_tensor(v_st[:, kv % 2, :, HEAD_DIM:2 * HEAD_DIM], src, hi.bitcast(F32),
                                        ALU.subtract).then_inc(v_split, 1)

            def double_keys(j):
                kc, kv, is_a = head_columns(j)[1], *head_columns(j)[4:6]
                pool.wait_ge(rope_added, chunk_end(ropes, heads_chunk(j, "k")))
                if kv:
                    before = max(i for i in range(j) if own_kv[i])
                    pool.wait_ge(t_written, t_count[("r", before)] + 1)
                out = k_two[:].rearrange("p t (n d) -> p t n d", n=2)
                nc.gpsimd.tensor_scalar(out, h[:, :, None, kc:kc + HEAD_DIM].to_broadcast([P, TILES, 2, HEAD_DIM]),
                                        1.0, 0.0, ALU.mult, ALU.add).then_inc(keys_doubled, 1)

            def scale(u):
                j, k = divmod(u, UNITS)
                pool.wait_ge(den_inverted, u + 1)
                rows = [(k, 0, SEQ)] if k < QT else [(QT + t, t * DEC_SEQ, (t + 1) * DEC_SEQ) for t in range(ST)]
                for t, a, z in rows:
                    s = prob[:, u % PRING, a:z]
                    ins = nc.gpsimd.tensor_scalar(s, s, den[:, j % 2, t:t + 1], 0.5, ALU.mult, ALU.mult)
                ins.then_inc(scaled, 1)

            def mixed_low(n):
                e = split_order[n]
                pool.wait_ge(mix_hi, n + 1)
                nc.gpsimd.tensor_tensor(t_lo[:, e, :], mix_t[:, e, :], t_hi[:, e, :].bitcast(F32), ALU.subtract) \
                    .then_inc(mix_lo_pool, 1)

            pool.wait_ge(pool_consts, 1)
            for g in range(4):
                weights_low(g)
            for t in range(TILES):
                for g in slices_at(0, t):
                    weights_low(g)
                square(0, t)
                if t:
                    head_power(0, t - 1)
            head_power(0, TILES - 1)
            head_rstd(0)

            def beside_projection(c, n):
                for g in slices_at(c, n):
                    weights_low(g)
                if kind_of(c) == NORM:
                    square(c, n)
                    if n:
                        head_power(c, n - 1)
                if kind_of(c - 1) == NORM:
                    for t in late_tiles(c, n):
                        add_rotation(c - 1, t)
                if kind_of(c) == NORM and n == TILES - 1:
                    head_power(c, n)
                    head_rstd(c)
                if kind_of(c) == ROPE:
                    add_rotation(c, n)

            for item in alone:
                beside_projection(*item)
            double_keys(0)
            for item in first_items:
                beside_projection(*item)
            split_values(0)
            for u in range(STEPS):
                j, k = divmod(u, UNITS)
                if 1 <= u < NU + 1:
                    scale(u - 1)
                for item in items_at(u):
                    beside_projection(*item)
                if j + 1 < HEADS and own_kv[j + 1] and k == 0:
                    double_keys(j + 1)
                if 0 < j < HEADS and own_kv[j] and k == 2:
                    split_values(j)
                if split_at.get(u, 0) >= N_HEADS_A // 2:
                    mixed_low(split_order.index(split_at[u]))
            for g in range((IN_CHUNKS + 1) * SLICES, CHUNKS * SLICES):
                weights_low(g)

            def scale_second_half(t):
                pool.wait_ge(ln_normed, 2 * t + 1)
                r = h[:, t, 512:D_MODEL]
                nc.gpsimd.tensor_tensor(r, r, h[:, 1, 2 * WIDTH_A:3 * WIDTH_A], ALU.mult).then_inc(ln_scaled, 1)

            pool.wait_ge(ln_loaded, 64)
            for t in range(TILES):
                pool.wait_ge(stats_ready, t + 1)
                mean, rstd_t, shift, v, y = mv[:, t, 0:1], *(lnr[:, t, k:k + 1] for k in range(4))
                after(nc.gpsimd.tensor_scalar(v, mv[:, t, 1:2], 1.0, LN_EPS, ALU.mult, ALU.add))
                after(nc.gpsimd.tensor_tensor(y, v, half[:, 0:1], ALU.pow))
                after(nc.gpsimd.tensor_scalar(rstd_t, y, y, v, ALU.mult, ALU.mult))
                after(nc.gpsimd.tensor_scalar(rstd_t, rstd_t, -0.5, 1.5, ALU.mult, ALU.add))
                after(nc.gpsimd.tensor_tensor(rstd_t, rstd_t, y, ALU.mult))
                nc.gpsimd.tensor_scalar(shift, mean, rstd_t, -1.0, ALU.mult, ALU.mult).then_inc(ln_rstd, 1)
                scale_second_half(t)


def kernel(**inputs):
    import concourse.bacc as bacc
    from concourse.bass_utils import run_bass_kernel_spmd

    nc = bacc.Bacc("TRN2", target_bir_lowering=False, num_devices=1, dynamic_dma_scratch_size=1024)
    arrays = {
        "x_prompt": np.ascontiguousarray(inputs["x_prompt"][0]),
        "x_sample": np.ascontiguousarray(inputs["x_sample"][0]),
        "w_in": np.ascontiguousarray(inputs["w_in"][0]),
        "w_out": np.ascontiguousarray(inputs["w_out"][0]),
        "q_norm": np.ascontiguousarray(inputs["q_norm"][0]),
        "k_norm": np.ascontiguousarray(inputs["k_norm"][0]),
        "ln_g": np.ascontiguousarray(inputs["ln_g"][0]),
        "ln_b": np.ascontiguousarray(inputs["ln_b"][0]),
        "consts": shape_constants(),
    }
    args = [nc.dram_tensor(n, a.shape, F32, kind="ExternalInput").ap() for n, a in arrays.items()]
    args += [nc.dram_tensor(n, (s, D_MODEL), F32, kind="ExternalOutput").ap()
             for n, s in (("y_prompt", SEQ), ("y_sample", DEC_SEQ))]
    build(nc, *args)
    r = run_bass_kernel_spmd(nc, [arrays], core_ids=[0])
    return (r.results[0]["y_prompt"].reshape(1, SEQ, D_MODEL), r.results[0]["y_sample"].reshape(1, DEC_SEQ, D_MODEL))
```
